# Optimizing a Trainium2 kernel written in Bass

```python
import jax, jax.numpy as jnp
from jax import lax
import numpy as np

D_MODEL = 2048
BATCH = 1
SEQ = 256
DEPTH = 1
DEC_BATCH = 8
DEC_SEQ = 1
PAST_LEN = 1024
PAGE_SIZE = 128

D_MIX = D_MODEL
D_ATT = D_MIX // 2
HD_ATT = 64
H_ATT = D_ATT // HD_ATT
DIL_PATTERNS = ((128, 1), (512, 4), (2048, 16))
WIN_MAX = max(w for w, _ in DIL_PATTERNS)
ATT_BLOCK = max(w // d for w, d in DIL_PATTERNS)
D_GLA_V = D_MIX - D_ATT
H_GLA = 4
D_GLA_K = D_GLA_V // 2
DK_GLA = D_GLA_K // H_GLA
DV_GLA = D_GLA_V // H_GLA
GATE_RANK = 16
GATE_TAU = 16.0
GLA_CHUNK = 64
D_FF = ((8 * D_MODEL // 3 + 255) // 256) * 256
NORM_EPS = 1e-6
PROJ_SIZES = (D_ATT, D_ATT, D_ATT, D_GLA_K, D_GLA_K, D_GLA_V, D_GLA_V, GATE_RANK)
D_PROJ = sum(PROJ_SIZES)

kernel_name = "hymba_dilated_gla_macaron_step"

def _rms_f32(x):
    xf = x.astype(jnp.float32)
    return xf * lax.rsqrt(jnp.mean(xf * xf, axis=-1, keepdims=True) + NORM_EPS)

def rmsnorm(x, g):
    return (_rms_f32(x) * g.astype(jnp.float32)).astype(x.dtype)

def swiglu(h, w_in, w_out):
    a, b = jnp.split(h @ w_in, 2, axis=-1)
    return (jax.nn.silu(a) * b) @ w_out

def project(h, w_in, w_gate2, b_gate2):
    B, T, _ = h.shape
    idx = [int(i) for i in np.cumsum(PROJ_SIZES)[:-1]]
    qa, ka, va, qg, kg, vg, rg, lr = jnp.split(h @ w_in, idx, axis=-1)
    qa = qa.reshape(B, T, H_ATT, HD_ATT)
    ka = ka.reshape(B, T, H_ATT, HD_ATT)
    va = va.reshape(B, T, H_ATT, HD_ATT)
    qg = qg.astype(jnp.float32).reshape(B, T, H_GLA, DK_GLA) * (DK_GLA ** -0.5)
    kg = kg.astype(jnp.float32).reshape(B, T, H_GLA, DK_GLA)
    vg = vg.astype(jnp.float32).reshape(B, T, H_GLA, DV_GLA)
    log_a = jax.nn.log_sigmoid((lr @ w_gate2 + b_gate2).astype(jnp.float32)) / GATE_TAU
    log_a = log_a.reshape(B, T, H_GLA, DK_GLA)
    return qa, ka, va, qg, kg, vg, rg, log_a

def dilated_attn_prompt(q, k, v, window, dil):
    B, S, H, Dh = q.shape
    n_keys = window // dil
    L = -(-S // dil)
    L = -(-L // ATT_BLOCK) * ATT_BLOCK
    Sp = L * dil
    nb = L // ATT_BLOCK

    def to_streams(a):
        a = jnp.pad(a, ((0, 0), (0, Sp - S), (0, 0), (0, 0)))
        a = a.reshape(B, L, dil, H, Dh).transpose(0, 2, 1, 3, 4)
        return a.reshape(B, dil, nb, ATT_BLOCK, H, Dh)

    def with_prev(a):
        prev = jnp.pad(a, ((0, 0), (0, 0), (1, 0), (0, 0), (0, 0), (0, 0)))[:, :, :-1]
        return jnp.concatenate([prev, a], axis=3)

    qs = to_streams(q)
    kk = with_prev(to_streams(k))
    vv = with_prev(to_streams(v))
    s = jnp.einsum("brnqhd,brnkhd->brnhqk", qs, kk) * (Dh ** -0.5)
    qi = jnp.arange(ATT_BLOCK)[:, None]
    ki = jnp.arange(2 * ATT_BLOCK)[None, :]
    dist = qi + ATT_BLOCK - ki
    band = (dist >= 0) & (dist <= n_keys)
    blk = jnp.arange(nb)[:, None, None]
    exists = (blk * ATT_BLOCK + ki[None] - ATT_BLOCK) >= 0
    mask = band[None] & exists
    s = jnp.where(mask[:, None], s, -jnp.inf)
    m = jnp.max(s, axis=-1, keepdims=True)
    e = jnp.exp(s - m)
    den = jnp.sum(e, axis=-1, keepdims=True)
    o = jnp.einsum("brnhqk,brnkhd->brnqhd", e / den, vv)
    lse = (m + jnp.log(den))[..., 0].transpose(0, 1, 2, 4, 3)
    o = o.reshape(B, dil, L, H, Dh).transpose(0, 2, 1, 3, 4).reshape(B, Sp, H, Dh)[:, :S]
    lse = lse.reshape(B, dil, L, H).transpose(0, 2, 1, 3).reshape(B, Sp, H)[:, :S]
    return o, lse

def dilated_attn_sample(q, kc, vc, window, dil):
    B, T, H, Dh = q.shape
    WB = kc.shape[1] - T
    j = jnp.arange(window // dil + 1)
    idx = WB + jnp.arange(T)[:, None] - dil * j[None, :]
    valid = idx >= 0
    idx = jnp.maximum(idx, 0)
    kg = kc[:, idx]
    vg = vc[:, idx]
    s = jnp.einsum("bthd,btjhd->bthj", q, kg) * (Dh ** -0.5)
    s = jnp.where(valid[None, :, None, :], s, -jnp.inf)
    m = jnp.max(s, axis=-1, keepdims=True)
    e = jnp.exp(s - m)
    den = jnp.sum(e, axis=-1, keepdims=True)
    o = jnp.einsum("bthj,btjhd->bthd", e / den, vg)
    return o, (m + jnp.log(den))[..., 0]

def combine_by_denominator(outs, lses):
    w = jax.nn.softmax(jnp.stack(lses, axis=0), axis=0)
    return jnp.sum(w[..., None] * jnp.stack(outs, axis=0), axis=0)

def dilated_mix_prompt(q, k, v):
    q, k, v = (a.astype(jnp.float32) for a in (q, k, v))
    outs, lses = [], []
    for window, dil in DIL_PATTERNS:
        o, lse = dilated_attn_prompt(q, k, v, window, dil)
        outs.append(o)
        lses.append(lse)
    return combine_by_denominator(outs, lses)

def dilated_mix_sample(q, kc, vc):
    q, kc, vc = (a.astype(jnp.float32) for a in (q, kc, vc))
    outs, lses = [], []
    for window, dil in DIL_PATTERNS:
        o, lse = dilated_attn_sample(q, kc, vc, window, dil)
        outs.append(o)
        lses.append(lse)
    return combine_by_denominator(outs, lses)

def gla_chunked(q, k, v, log_a, s0):
    B, T, H, K = q.shape
    C = GLA_CHUNK
    nc = T // C
    causal = jnp.tril(jnp.ones((C, C), dtype=bool))

    def to_chunks(a):
        return a.reshape(B, nc, C, H, a.shape[-1]).transpose(1, 0, 3, 2, 4)

    def step(S, inp):
        qc, kc, vc, gc = inp
        b = jnp.cumsum(gc, axis=2)
        o_inter = jnp.einsum("bhck,bhkv->bhcv", qc * jnp.exp(b), S)
        diff = b[:, :, :, None, :] - b[:, :, None, :, :]
        decay = jnp.exp(jnp.where(causal[:, :, None], diff, -jnp.inf))
        A = jnp.einsum("bhtk,bhsk,bhtsk->bhts", qc, kc, decay)
        o = o_inter + jnp.einsum("bhts,bhsv->bhtv", A, vc)
        bl = b[:, :, -1:, :]
        S = jnp.exp(bl[:, :, 0, :])[..., None] * S + jnp.einsum("bhsk,bhsv->bhkv", kc * jnp.exp(bl - b), vc)
        return S, o

    S, o = lax.scan(step, s0, (to_chunks(q), to_chunks(k), to_chunks(v), to_chunks(log_a)))
    o = o.transpose(1, 0, 3, 2, 4).reshape(B, T, H, v.shape[-1])
    return o, S

def gla_recurrent(q, k, v, log_a, s0):
    def step(S, inp):
        qt, kt, vt, gt = inp
        S = jnp.exp(gt)[..., None] * S + kt[..., :, None] * vt[..., None, :]
        return S, jnp.einsum("bhk,bhkv->bhv", qt, S)

    xs = tuple(a.transpose(1, 0, 2, 3) for a in (q, k, v, log_a))
    S, o = lax.scan(step, s0, xs)
    return o.transpose(1, 0, 2, 3), S

def merge(o_att, o_gla, r_g, g_att_out, g_gla_out, w_out, dtype):
    B, T = o_att.shape[:2]
    a = _rms_f32(o_att.reshape(B, T, D_ATT)) * g_att_out.astype(jnp.float32)
    gg = _rms_f32(o_gla) * g_gla_out.astype(jnp.float32)
    gg = gg.reshape(B, T, D_GLA_V) * jax.nn.silu(r_g.astype(jnp.float32))
    return jnp.concatenate([a, gg], axis=-1).astype(dtype) @ w_out

def setup_inputs(seed: int = 0) -> dict:
    key = jax.random.key(seed)
    ks = jax.random.split(key, 24)
    f32 = jnp.float32
    WB = min(WIN_MAX, PAST_LEN)
    nrm = lambda k, shape, s: jax.random.normal(k, shape, f32) * s
    gain = lambda k, shape: 1.0 + 0.02 * jax.random.normal(k, shape, f32)
    return {
        "x_prompt": nrm(ks[0], (BATCH, SEQ, D_MODEL), 1.0),
        "x_sample": nrm(ks[1], (DEC_BATCH, DEC_SEQ, D_MODEL), 1.0),
        "cache_att_k": nrm(ks[2], (DEPTH, DEC_BATCH, WB, H_ATT, HD_ATT), 1.0),
        "cache_att_v": nrm(ks[3], (DEPTH, DEC_BATCH, WB, H_ATT, HD_ATT), 1.0),
        "state_gla": nrm(ks[4], (DEPTH, DEC_BATCH, H_GLA, DK_GLA, DV_GLA), 2.0),
        "g_ffn1": gain(ks[5], (DEPTH, D_MODEL)),
        "w_ffn1_in": nrm(ks[6], (DEPTH, D_MODEL, 2 * D_FF), D_MODEL ** -0.5),
        "w_ffn1_out": nrm(ks[7], (DEPTH, D_FF, D_MODEL), D_FF ** -0.5),
        "g_mix": gain(ks[8], (DEPTH, D_MODEL)),
        "w_in": nrm(ks[9], (DEPTH, D_MODEL, D_PROJ), D_MODEL ** -0.5),
        "w_gate2": nrm(ks[10], (DEPTH, GATE_RANK, D_GLA_K), GATE_RANK ** -0.5),
        "b_gate2": nrm(ks[11], (DEPTH, D_GLA_K), 0.1),
        "g_att_out": gain(ks[12], (DEPTH, D_ATT)),
        "g_gla_out": gain(ks[13], (DEPTH, DV_GLA)),
        "w_out": nrm(ks[14], (DEPTH, D_MIX, D_MODEL), D_MIX ** -0.5),
        "g_ffn2": gain(ks[15], (DEPTH, D_MODEL)),
        "w_ffn2_in": nrm(ks[16], (DEPTH, D_MODEL, 2 * D_FF), D_MODEL ** -0.5),
        "w_ffn2_out": nrm(ks[17], (DEPTH, D_FF, D_MODEL), D_FF ** -0.5),
        "g_final": gain(ks[18], (D_MODEL,)),
    }

def reference(x_prompt, x_sample, cache_att_k, cache_att_v, state_gla, g_ffn1, w_ffn1_in, w_ffn1_out,
              g_mix, w_in, w_gate2, b_gate2, g_att_out, g_gla_out, w_out, g_ffn2, w_ffn2_in, w_ffn2_out,
              g_final):
    xp, xs = x_prompt, x_sample
    S_p = xp.shape[1]
    T_s = xs.shape[1]
    wb_p = min(WIN_MAX, S_p)
    nk_p, nv_p, ns_p, nk_s, nv_s, ns_s = [], [], [], [], [], []
    for l in range(DEPTH):
        xp = xp + 0.5 * swiglu(rmsnorm(xp, g_ffn1[l]), w_ffn1_in[l], w_ffn1_out[l])
        xs = xs + 0.5 * swiglu(rmsnorm(xs, g_ffn1[l]), w_ffn1_in[l], w_ffn1_out[l])

        qa, ka, va, qg, kg, vg, rg, la = project(rmsnorm(xp, g_mix[l]), w_in[l], w_gate2[l], b_gate2[l])
        o_att = dilated_mix_prompt(qa, ka, va)
        s0 = jnp.zeros((xp.shape[0], H_GLA, DK_GLA, DV_GLA), jnp.float32)
        o_gla, s_fin = gla_chunked(qg, kg, vg, la, s0)
        xp = xp + merge(o_att, o_gla, rg, g_att_out[l], g_gla_out[l], w_out[l], xp.dtype)
        nk_p.append(ka[:, S_p - wb_p:])
        nv_p.append(va[:, S_p - wb_p:])
        ns_p.append(s_fin.astype(xp.dtype))

        qa, ka, va, qg, kg, vg, rg, la = project(rmsnorm(xs, g_mix[l]), w_in[l], w_gate2[l], b_gate2[l])
        kc = jnp.concatenate([cache_att_k[l].astype(ka.dtype), ka], axis=1)
        vc = jnp.concatenate([cache_att_v[l].astype(va.dtype), va], axis=1)
        o_att = dilated_mix_sample(qa, kc, vc)
        o_gla, s_new = gla_recurrent(qg, kg, vg, la, state_gla[l].astype(jnp.float32))
        xs = xs + merge(o_att, o_gla, rg, g_att_out[l], g_gla_out[l], w_out[l], xs.dtype)
        nk_s.append(ka)
        nv_s.append(va)
        ns_s.append(s_new.astype(state_gla.dtype))

        xp = xp + 0.5 * swiglu(rmsnorm(xp, g_ffn2[l]), w_ffn2_in[l], w_ffn2_out[l])
        xs = xs + 0.5 * swiglu(rmsnorm(xs, g_ffn2[l]), w_ffn2_in[l], w_ffn2_out[l])

    y_prompt = rmsnorm(xp, g_final)
    y_sample = rmsnorm(xs, g_final)
    return (y_prompt, y_sample, jnp.stack(nk_p), jnp.stack(nv_p), jnp.stack(ns_p),
            jnp.stack(nk_s), jnp.stack(nv_s), jnp.stack(ns_s))


_drawn_inputs = setup_inputs


def setup_inputs(seed=0):
    import zlib

    import numpy as np

    out = dict(_drawn_inputs(seed))
    spreads = {}
    factors = {'g_ffn1': 4.832, 'g_att_out': 5.309, 'g_gla_out': 7.575, 'g_ffn2': 8.0, 'g_final': 2.838}
    for name, (base, spread) in spreads.items():
        noise = np.random.default_rng([zlib.crc32(name.encode()), seed]).standard_normal(out[name].shape)
        drawn = base * np.exp(spread * noise) if base else spread * noise
        out[name] = __import__('jax').numpy.asarray(drawn.astype(out[name].dtype))
    for name, factor in factors.items():
        out[name] = (out[name] * factor).astype(out[name].dtype)
    return out
```

```python
from contextlib import ExitStack

import concourse.bass as bass
from concourse import mybir

F32 = mybir.dt.float32
F32R = mybir.dt.float32r
U8 = mybir.dt.uint8
ACT = mybir.ActivationFunctionType
ALU = mybir.AluOpType
AX_X = mybir.AxisListType.X

P = 128
D = 2048
KT = D // P
TP, TS = 256, 8
T = TP + TS
D_FF = 5632
FT = D_FF // P
D_ATT, H_ATT, HD = 1024, 16, 64
AT_T = D_ATT // P
H_GLA, DK, DV = 4, 128, 256
D_GK, D_GV = H_GLA * DK, H_GLA * DV
RANK = 16
TAU = 16.0
EPS = 1e-6
PAST = 1024
PATTERNS = ((128, 1), (512, 4), (2048, 16))
CQ, CK, CV = 0, D_ATT, 2 * D_ATT
CQG = 3 * D_ATT
CKG = CQG + D_GK
CVG = CKG + D_GK
CRG = CVG + D_GV
CLR = CRG + D_GV
NEG = -1.0e38

RING = 4
CK_T, CN_T = 2, 4
CW = CN_T * P
FI_BLOCKS = D_FF // CW
FI_BODY = 2 * KT // CK_T
FO_BLOCKS = D // CW
FO_CH = FT // CK_T
FI1 = 0
FO1 = FI1 + FI_BLOCKS * FI_BODY
MIX = FO1 + FO_BLOCKS * FO_CH

BLOCKS = [(CKG, "kg", 0), ("lr", None, None), (CQG, "qg", 0), (CVG, "vg", 0), (CVG + CW, "vg", 4),
          (CQ, "qa", 0), (CK, "ka", 0), (CV, "va", 0), (CQ + CW, "qa", 4), (CK + CW, "ka", 4),
          (CV + CW, "va", 4), (CRG, "rg", 0), (CRG + CW, "rg", 4)]
IN_CH = KT // CK_T
OUT_CH = IN_CH // 2


def mixer_chunks():
    out = []
    for m, (col, _, _) in enumerate(BLOCKS):
        n = 2 if col == "lr" else IN_CH
        out += [("lr" if col == "lr" else "in", m, j, j == n - 1) for j in range(n)]
    for half in ("gla", "att"):
        for q in range(FO_BLOCKS):
            out += [(half, q, j, j == OUT_CH - 1) for j in range(OUT_CH)]
    return out


CHUNKS = mixer_chunks()
FI2 = MIX + len(CHUNKS)
FO2 = FI2 + FI_BLOCKS * FI_BODY
END = FO2 + FO_BLOCKS * FO_CH
assert (FO_CH * 2) % RING == 0 and FI_BODY % RING == 0


def block_tiles():
    before, n = {}, 0
    for kind, m, j, _ in CHUNKS:
        if j == 0 and kind != "lr":
            before[kind, m] = n
            n += CN_T
    return before, n


TILES_BEFORE, MIX_TILES = block_tiles()


def end_slot(kind, m):
    return max(i for i, (k, b, _, _) in enumerate(CHUNKS) if (k, b) == (kind, m))


LEVELS = (128, 64, 32, 16, 8, 4, 2, 1)


def mixer_plan():
    plan = {}

    def put(slot, *step):
        plan.setdefault(slot, []).append(step)

    by_buf = {(b, t): end_slot("in", m) for m, (_, b, t) in enumerate(BLOCKS) if b}
    lr = end_slot("lr", 1)
    put(2, "mean", "mix")
    put(lr, "lowrank", 0)
    put(lr + 2, "gate", 0)
    put(lr + 6, "cum", 0)
    put(lr + 7, "cum", 1)
    for g in range(2):
        for part in range(3):
            put(by_buf["vg", 4 * g] + 2 + part, "nat", ("vg", part, g))
    s = by_buf["qg", 0] + 1
    for n in range(len(LEVELS)):
        put(s + 2 * n, "level_in", n)
        put(s + 2 * n + 1, "level_out", n)
    s += 2 * len(LEVELS)
    put(s, "kdecay", 0)
    put(s + 1, "level_out", len(LEVELS))
    s = max(s + 2, by_buf["vg", 4] + 5)
    put(s, "kd_nat", 0)
    put(s + 1, "kd_nat", 1)
    for h in range(H_GLA):
        put(s + 1 + h, "gla_out", h)
    put(s + 4, "state", 0)
    put(s + 5, "state", 1)
    assert s + 7 < by_buf["va", 0]
    s += 12
    for b in range(TS):
        put(s + 2 * b, "rec", b)
        put(s + 3 + 2 * b, "rec_out", b)
    rec_end = s + 3 + 2 * (TS - 1)
    for grp in range(2):
        s = by_buf["va", 4 * grp] + 2
        put(s, "nat", ("va", 0, grp))
        put(s + 1, "nat", ("va", 1, grp))
        put(s + 2, "nat", ("ka", 0, grp))
        put(s + 3, "nat", ("ka", 1, grp))
        put(s + 4, "nat", ("va", 2, grp))
        put(s + 5, "nat", ("ka", 2, grp))
        put(by_buf["qa", 4 * grp] + 2, "nat", ("qa", 2, grp))
        for i in range(H_ATT // 2):
            h = H_ATT // 2 * grp + i
            put(s + 2 * i, "score", h)
            put(s + 2 * i + 2, "probs_t", h)
            put(s + 2 * i + 4, "values", h)
            if h % 2:
                put(s + 2 * i + 5, "att_split", h // 2)
    s = max(rec_end, by_buf["qa", 4] + 2) + 3
    for b in range(TS):
        put(s + 3 * b, "cache_k", b)
    s += 3 * TS
    put(s, "self_score", 0)
    put(s + 1, "s_scores", 0)
    put(s + 4, "s_probs", 0)
    put(s + 6, "s_values", 0)
    for b in range(TS):
        put(s + 6 + b // 2, "s_value", b)
    put(s + 10, "own_value", 0)
    put(s + 11, "att_split_s", 0)
    put(s + 12, "mean_att", 0)
    assert s + 11 < end_slot("gla", FO_BLOCKS - 1), s
    g = by_buf["rg", 0] - 6
    assert g > rec_end + 1
    for h in range(H_GLA):
        put(g, "gla_sq", h)
        put(g + 1 + h, "gla_mean", h)
    put(by_buf["rg", 0] + 1, "gla_gate", 0)
    put(by_buf["rg", 0] + 2, "gla_split", 0)
    put(by_buf["rg", 4], "gla_gate", 1)
    put(by_buf["rg", 4], "gla_split", 1)
    return {k: plan[k] for k in sorted(plan)}


PLAN = mixer_plan()
S_ROWS = [arg[::2] for steps in PLAN.values() for step, arg in steps if step == "nat" and arg[1] == 2]
BANKS = {"mean": (0,), "lowrank": (1,), "gate": (0, 1, 2), "cum": (0,), "nat": (3,),
         "level_out": (1, 2), "gla_out": (0,), "kd_nat": (3,), "state": (1,), "rec_out": (3,),
         "score": (0,), "probs_t": (1,), "values": (2,), "s_scores": (3,),
         "s_probs": (3,), "s_values": (3,), "mean_att": (0,), "gla_mean": (3,)}


def cache_count(b, t, is_value):
    return 16 * (1 + t) * ((TS // 2 if is_value else 0) + b // 2 + 1)


def uses_of_banks():
    uses, count = {}, [0] * 4
    for steps in PLAN.values():
        for step, arg in steps:
            for n, bank in enumerate(BANKS.get(step, ())):
                uses[step, arg, n] = (bank, count[bank])
                count[bank] += 1
    return uses, count


USE, USES = uses_of_banks()


def layer_step(nc, x_prompt, x_sample, cache_k, cache_v, state, g_ffn1, w1_in, w1_out, g_mix, w_in,
               w_gate2, b_gate2, g_att, g_gla, w_out, g_ffn2, w2_in, w2_out, g_final,
               c_ident, c_ones, c_cum, c_level, c_mult, c_mask, c_smult,
               y_p, y_s, nk_p, nv_p, ns_p, nk_s, nv_s, ns_s):
    rows_q = nc.dram_tensor("rows_q", (TS, D_ATT), F32, kind="Internal").ap()
    rows_v = nc.dram_tensor("rows_v", (TS, D_GV), F32, kind="Internal").ap()
    with ExitStack() as ctx:
        base = (nc.sbuf_base + 63) // 64 * 64
        ctx.enter_context(nc.sbuf_tensor("arena", [P, (212800 - 64) // 4], F32))

        def at(name, offset, shape, dt=F32):
            return nc.alloc_sbuf_tensor_at(name, [P, *shape], dt, offset=base + offset)

        here = [0]

        def sb(name, shape, dt=F32):
            size = 1 if dt == U8 else 4
            for n in shape:
                size *= n
            t = at(name, here[0], shape, dt)
            here[0] += (size + 31) // 32 * 32
            return t

        x = sb("x", [KT, T])
        xh, xl = sb("xh", [KT, T], F32R), sb("xl", [KT, T], F32R)
        raw = sb("raw", [RING, CK_T, CW])
        wh, wl = sb("wh", [RING, CK_T, CW], F32R), sb("wl", [RING, CK_T, CW], F32R)
        ident = sb("ident", [P])
        ones = sb("ones", [4, 1])
        eps = sb("eps", [1])
        ssq = sb("ssq", [T])
        rstd = sb("rstd", [T])
        asq = sb("asq", [T])
        root = sb("root", [T])
        gains = sb("gains", [4, KT])
        gatt = sb("gatt", [AT_T])
        ggla = sb("ggla", [DV // P])
        sc_s = sb("sc_s", [2, H_ATT, TS])
        sm_s = sb("sm_s", [257])
        smult = sb("smult", [257])
        pt_s = sb("pt_s", [2, H_ATT, TS])
        tiny = sb("tiny", [64])
        a_s = sb("a_s", [H_GLA, TS])
        s_start = here[0]
        s_buf = sb("s_buf", [4, T])
        t_buf = sb("t_buf", [4, T])
        u_at = here[0]
        uh, ul = sb("uh", [FT, T], F32R), sb("ul", [FT, T], F32R)
        assert here[0] <= 212800 - 64, here[0]
        xn = at("xn", u_at, [2, D])
        xns = at("xns", u_at + 2 * D * 4, [D])
        here[0] = u_at
        proj = {name: sb(name, [n, T]) for name, n in
                (("qa", AT_T), ("ka", AT_T), ("va", AT_T), ("qg", H_GLA), ("kg", H_GLA), ("vg", AT_T),
                 ("rg", AT_T))}
        og = proj["vg"]
        rg = proj["rg"]
        lowr = sb("lowr", [T])
        wg2 = sb("wg2", [D_GK])
        work = here[0]
        la = sb("la", [2, D_GK])
        cum = sb("cum", [H_GLA, TP])
        dif = sb("dif", [H_GLA, TP])
        qe, ke = sb("qe", [H_GLA, TP]), sb("ke", [H_GLA, TP])
        am = sb("am", [H_GLA, 3 * P])
        vgn = sb("vgn", [2, D_GV])
        cumw = sb("cumw", [TP])
        level = sb("level", [len(LEVELS), P], U8)
        assert here[0] <= u_at + 2 * FT * T * 4
        level_f = at("level_f", here[0], [len(LEVELS), P])
        kdn = at("kdn", work, [2, D_GK])
        sfin = at("sfin", work + 2 * 4096, [H_GLA, DV])
        here[0] = work
        van = sb("van", [2, D_ATT])
        sm = sb("sm", [3 * P])
        pt = sb("pt", [3 * P])
        mult, mask = sb("mult", [3 * P]), sb("mask", [3 * P])
        stream = sb("stream", [4, 1024])
        bcast = sb("bcast", [1024])
        prod = sb("prod", [1024])
        assert here[0] <= u_at + 2 * FT * T * 4
        rows = at("rows", s_start, [2, 512])
        rows_s = at("rows_s", s_start + 4096, [2, 512])
        sqg = at("sqg", u_at + 3 * AT_T * T * 4, [H_GLA, T])
        rstdg = at("rstdg", u_at + (3 * AT_T + H_GLA) * T * 4, [H_GLA, T])
        gh = at("gh", u_at + 3 * AT_T * T * 4, [AT_T, T], F32R)
        gl = at("gl", u_at + (4 * AT_T + 2 * H_GLA) * T * 4, [AT_T, T], F32R)
        ath = at("ath", u_at + AT_T * T * 4, [AT_T, T], F32R)
        atl = at("atl", u_at + 2 * AT_T * T * 4, [AT_T, T], F32R)
        yn = at("yn", KT * T * 4, [2, D])
        yns = at("yns", KT * T * 4 + 2 * D * 4, [D])

        g0 = ctx.enter_context(nc.psum_tensor("g0", [P, 4, 512], F32))
        g1 = ctx.enter_context(nc.psum_tensor("g1", [P, 4, 512], F32))
        groups = (g0, g1)

        names = {}

        def sem(name):
            names[name] = ctx.enter_context(nc.semaphore(name))
            return names[name]


        raw_full = [sem(f"raw_full{i}") for i in range(RING)]
        hi_done = sem("hi_done")
        lo_done = sem("lo_done")
        used = sem("used")
        consts_in, x_in, xs_in = sem("consts_in"), sem("x_in"), sem("xs_in")
        glac_in, attc_in, wg2_in = sem("glac_in"), sem("attc_in"), sem("wg2_in")
        x_turned = sem("x_turned")
        x_new = sem("x_new")
        xh_new, xl_new = sem("xh_new"), sem("xl_new")
        sq_new, sq_part, ssq_new = sem("sq_new"), sem("sq_part"), sem("ssq_new")
        mean_full, root_new, rstd_new = sem("mean_full"), sem("root_new"), sem("rstd_new")
        gate_in, gate_silu = sem("gate_in"), sem("gate_silu")
        up_in, u_new = sem("up_in"), sem("u_new")
        uh_new, ul_new = sem("uh_new"), sem("ul_new")
        tiles = sem("tiles")
        proj_new = sem("proj_new")
        full = [sem(f"bank_full{i}") for i in range(4)]
        free = [sem(f"bank_free{i}") for i in range(4)]
        vec = sem("vec")
        act_own = sem("act_own")
        lowr_new, gate_e, gate_l, la_new = sem("lowr_new"), sem("gate_e"), sem("gate_l"), sem("la_new")
        cum_new, dif_new, dec_new, qk_new = sem("cum_new"), sem("dif_new"), sem("dec_new"), sem("qk_new")
        am_new, kd_new, kdn_new, og_new = sem("am_new"), sem("kd_new"), sem("kdn_new"), sem("og_new")
        sfin_new, sfin_out = sem("sfin_new"), sem("sfin_out")
        rows_new, rows_out = sem("rows_new"), [sem(f"rows_out{i}") for i in range(2)]
        rowss_out = [sem(f"rowss_out{i}") for i in range(2)]
        rowq_out = sem("rowq_out")
        van_new, van_out = sem("van_new"), sem("van_out")
        st_in = [sem(f"st_in{i}") for i in range(4)]
        bc_in, outer_new, st_new, st_out = sem("bc_in"), sem("outer_new"), sem("st_new"), [sem(f"st_out{i}") for i in range(4)]
        rec_new = sem("rec_new")
        masked, e_new, p_new, pt_new, oatt_new = (sem("masked"), sem("e_new"), sem("p_new"),
                                                 sem("pt_new"), sem("oatt_new"))
        ath_new, atl_new = sem("ath_new"), sem("atl_new")
        kc_in = [sem(f"kc_in{i}") for i in range(4)]
        qb_in, prod_new, sc_new = sem("qb_in"), sem("prod_new"), sem("sc_new")
        self_new, smax_new, se_new, sp_new, pts_new, oatts_new = (
            sem("self_new"), sem("smax_new"), sem("se_new"), sem("sp_new"), sem("pts_new"), sem("oatts_new"))
        asq_new, amean_full, aroot_new, arstd_new = (sem("asq_new"), sem("amean_full"),
                                                    sem("aroot_new"), sem("arstd_new"))
        gsq_new, gss_new, groot_new, grstd_new = (sem("gsq_new"), sem("gss_new"), sem("groot_new"),
                                                  sem("grstd_new"))
        rg_silu, og_fin = sem("rg_silu"), sem("og_fin")
        fin_g, fin_turned, fin_rows = sem("fin_g"), sem("fin_turned"), sem("fin_rows")
        fmean_full, froot, frstd, y_new, y_out = (sem("fmean_full"), sem("froot"), sem("frstd"),
                                                  sem("y_new"), sem("y_out"))
        a_exp = sem("a_exp")
        misc = sem("misc")

        gh_new, v_used, cleared = sem("gh_new"), sem("v_used"), sem("cleared")
        stored, eps_set, sconst_in = sem("stored"), sem("eps_set"), sem("sconst_in")

        def taken(eng, step, arg, n=0):
            bank, k = USE[step, arg, n]
            eng.wait_ge(free[bank], k + 1)

        def filled(eng, step, arg, n=0):
            bank, k = USE[step, arg, n]
            eng.wait_ge(full[bank], k + 1)
            return g1[:, bank, :], free[bank]

        block = ctx.enter_context(nc.Block())

        @block.sync
        def _(sp):
            def load(c, slot, src, shape=None):
                sp.wait_ge(lo_done, c + 1)
                dst = raw[:, slot, :, :]
                if shape:
                    dst = dst.rearrange("p a b -> p (a b)")[:, 0:shape[0] * shape[1]].rearrange(
                        "p (a b) -> p a b", a=shape[0])
                sp.dma_start(dst, src).then_inc(raw_full[slot], 16)

            def rows_of(w, k, n, cols):
                return w[k * P:(k + n) * P, cols].rearrange("(t p) n -> p t n", p=P)

            def ffn_in(w, c0):
                with sp.Fori(0, FI_BLOCKS) as i:
                    for k in range(FI_BODY):
                        j, up = k % (FI_BODY // 2), k // (FI_BODY // 2)
                        load(FI_BODY * i + (c0 + k), (c0 + k) % RING,
                             rows_of(w, CK_T * j, CK_T, bass.ds(CW * i + up * D_FF, CW)))

            def ffn_out_pairs(w, c0):
                with sp.Fori(0, FO_BLOCKS // 2) as i:
                    for k in range(2 * FO_CH):
                        b, j = k // FO_CH, k % FO_CH
                        load(2 * FO_CH * i + (c0 + k), (c0 + k) % RING,
                             rows_of(w, CK_T * j, CK_T, bass.ds(2 * CW * i + b * CW, CW)))

            for half in range(2):
                sp.dma_start(xn[:, half, :], x_prompt[0, half * P:(half + 1) * P, :]).then_inc(x_in, 16)
                if half == 0:
                    sp.dma_start(xns[0:TS, :], x_sample[:, 0, :]).then_inc(xs_in, 16)
            ffn_in(w1_in[0], FI1)
            ffn_out_pairs(w1_out[0], FO1)
            for n, (kind, m, j, _) in enumerate(CHUNKS):
                c = MIX + n
                if kind == "in":
                    src = rows_of(w_in[0], CK_T * j, CK_T, slice(BLOCKS[m][0], BLOCKS[m][0] + CW))
                    load(c, c % RING, src)
                elif kind == "lr":
                    load(c, c % RING, rows_of(w_in[0], KT // 2 * j, KT // 2, slice(CLR, CLR + RANK)),
                         (KT // 2, RANK))
                else:
                    k0 = (AT_T if kind == "gla" else 0) + CK_T * j
                    load(c, c % RING, rows_of(w_out[0], k0, CK_T, slice(m * CW, (m + 1) * CW)))
            ffn_in(w2_in[0], FI2)
            ffn_out_pairs(w2_out[0], FO2)
            sp.wait_ge(y_new, 3)
            for half in range(2):
                sp.dma_start(y_p[0, half * P:(half + 1) * P, :], yn[:, half, :]).then_inc(y_out, 16)
            sp.dma_start(y_s[:, 0, :], yns[0:TS, :]).then_inc(y_out, 16)
            sp.wait_ge(y_out, 48)

        @block.tensor
        def _(pe):
            def multiply(c, slot, rhs, out, first, last, before=None, tile_sems=False):
                pe.wait_ge(lo_done, c + (RING + 1))
                for n in range(CN_T):
                    if before:
                        before(n)
                    for k in range(CK_T):
                        a, b = rhs(k)
                        hi = wh[:, slot, k, n * P:(n + 1) * P]
                        lo = wl[:, slot, k, n * P:(n + 1) * P]
                        pe.matmul(out(n), hi, a, start=first and k == 0, stop=False)
                        pe.matmul(out(n), hi, b, start=False, stop=False)
                        mm = pe.matmul(out(n), lo, a, start=False, stop=last and k == CK_T - 1)
                    if tile_sems and n < CN_T - 1:
                        mm.then_inc(tiles, 1)
                mm.then_inc(used, 1)

            def mean(nth, done):
                pe.wait_ge(ssq_new, 4 * nth)
                pe.matmul(g1[:, 0, 0:T], ones[:, 1, :].to_broadcast([P, P]), ssq[:, :], start=True,
                          stop=True).then_inc(done, 1)

            def ffn_in(nth, c0):
                def body(i, first):
                    for k in range(FI_BODY):
                        j, up = k % (FI_BODY // 2), k // (FI_BODY // 2)
                        if k == 0 and not first:
                            pe.wait_ge(gate_in, i + FI_BLOCKS * nth)
                        if k == 0 and first:
                            if nth == 0:
                                pe.wait_ge(x_new, 3)
                            else:
                                pe.wait_ge(proj_new, MIX_TILES)
                        if first and k == 6:
                            if nth == 0:
                                pe.wait_ge(x_new, 4)
                            else:
                                for b in range(4):
                                    pe.wait_ge(free[b], USES[b])
                            mean(1 + 2 * nth, mean_full)
                        if k == FI_BODY // 2:
                            if first:
                                pe.wait_ge(root_new, 1 + nth)
                            else:
                                pe.wait_ge(up_in, i + FI_BLOCKS * nth)
                        if first and not up and j % 2 == 0:
                            pe.wait_ge(xl_new, 8 * nth + j // 2 + 1)
                        multiply(FI_BODY * i + (c0 + k), (c0 + k) % RING,
                                 lambda t: (xh[:, CK_T * j + t, :], xl[:, CK_T * j + t, :]),
                                 lambda n: groups[up][:, n, 0:T], j == 0, j == KT // CK_T - 1)
                body(0, True)
                with pe.Fori(1, FI_BLOCKS) as i:
                    body(i, False)

            def ffn_out_chunk(nth, c, q, j, slot):
                if j % 2 == 0:
                    pe.wait_ge(ul_new, FI_BLOCKS * nth + j // 2 + 1)
                multiply(c, slot, lambda t: (uh[:, CK_T * j + t, :], ul[:, CK_T * j + t, :]),
                         lambda n: groups[q % 2][:, n, 0:T], j == 0, j == FO_CH - 1)

            pe.wait_ge(consts_in, 16 * 8)
            for q in range(KT // 4):
                if q >= 2:
                    pe.wait_ge(x_new, q - 1)
                if q == 0:
                    pe.wait_ge(x_in, 32)
                    pe.wait_ge(xs_in, 16)
                for n in range(4):
                    f = slice((4 * q + n) * P, (4 * q + n + 1) * P)
                    g = groups[q % 2]
                    for half in range(2):
                        pe.transpose(g[:, n, half * P:(half + 1) * P], xn[:, half, f], ident[:, :])
                    mm = pe.transpose(g[:, n, TP:T], xns[0:TS, f], ident[0:TS, 0:TS])
                mm.then_inc(x_turned, 1)

            ffn_in(0, FI1)
            with pe.Fori(0, FO_BLOCKS // 2) as i:
                for k in range(2 * FO_CH):
                    b, j = k // FO_CH, k % FO_CH
                    if j == 0:
                        if b == 0:
                            pe.wait_ge(gate_in, FI_BLOCKS)
                            pe.wait_ge(x_new, 2 * i + 3)
                        else:
                            pe.wait_ge(up_in, FI_BLOCKS)
                            pe.wait_ge(x_new, 2 * i + 4)
                    ffn_out_chunk(0, 2 * FO_CH * i + (FO1 + k), b, j, (FO1 + k) % RING)

            def fill(step, arg, n=0):
                bank, k = USE[step, arg, n]
                if k:
                    pe.wait_ge(free[bank], k)
                else:
                    pe.wait_ge(x_new, 8)
                return g1[:, bank, :], full[bank]

            NAT = {"vg": 0, "va": 1, "ka": 2, "qa": 3}

            def nat(name, half, grp):
                out, done = fill("nat", (name, half, grp))
                m = max(i for i, (_, b, t) in enumerate(BLOCKS) if (b, t) == (name, 4 * grp))
                pe.wait_ge(proj_new, TILES_BEFORE["in", m] + CN_T)
                cols, n = (slice(half * P, (half + 1) * P), P) if half < 2 else (slice(TP, T), TS)
                for t in range(4):
                    mm = pe.transpose(out[0:n, t * P:(t + 1) * P], proj[name][:, 4 * grp + t, cols],
                                      ident[:, :])
                mm.then_inc(done, 1)

            def gate(_):
                taken(pe, "lowrank", 0)
                pe.wait_ge(wg2_in, 32)
                for half in range(2):
                    out, done = fill("gate", 0, half)
                    pe.matmul(out[:, 0:D_GK], lowr[0:RANK + 1, half * P:(half + 1) * P],
                              wg2[0:RANK + 1, :], start=True, stop=True).then_inc(done, 1)
                out, done = fill("gate", 0, 2)
                for h in range(H_GLA):
                    mm = pe.matmul(out[:, h * TS:(h + 1) * TS], wg2[0:RANK + 1, h * DK:(h + 1) * DK],
                                   lowr[0:RANK + 1, TP:T], start=True, stop=True)
                mm.then_inc(done, 1)

            def cumulate(pair):
                out, done = fill("cum", pair)
                taken(pe, "gate", 0, 0)
                taken(pe, "gate", 0, 1)
                pe.wait_ge(glac_in, 32)
                for i in range(2):
                    h = slice((2 * pair + i) * DK, (2 * pair + i + 1) * DK)
                    o = out[:, i * TP:(i + 1) * TP]
                    pe.matmul(o, la[:, 0, h], cumw[:, :], start=True, stop=False, skip_group_check=True)
                    mm = pe.matmul(o[:, P:TP], la[:, 1, h], cumw[:, 0:P], start=False, stop=True,
                                   skip_group_check=True)
                mm.then_inc(done, 1)

            def level_out(n):
                if n < len(LEVELS):
                    pe.wait_ge(qk_new, n + 1)
                for half in range(2):
                    out, done = fill("level_out", n, half)
                    tok = slice(half * P, (half + 1) * P)
                    for i in range(2 if n == 0 else H_GLA):
                        if n == 0:
                            h = 2 * half + i
                            k, q = ke[:, h, 0:P], qe[:, h, P:TP]
                        elif n < len(LEVELS):
                            k, q = ke[:, i, tok], qe[:, i, tok]
                        else:
                            k, q = proj["kg"][:, i, tok], proj["qg"][:, i, tok]
                        mm = pe.matmul(out[:, i * P:(i + 1) * P], k, q, start=True, stop=True,
                                       skip_group_check=True)
                    mm.then_inc(done, 1)

            def gla_out(h):
                out, done = fill("gla_out", h)
                for i in range(2):
                    taken(pe, "level_out", 0, i)
                    taken(pe, "level_out", len(LEVELS), i)
                    for g in range(2):
                        taken(pe, "nat", ("vg", i, g))
                for t in range(2):
                    v = slice((2 * h + t) * P, (2 * h + t + 1) * P)
                    o = out[:, t * TP:(t + 1) * TP]
                    pe.matmul(o, vgn[:, 0, v], am[:, h, 0:TP], start=True, stop=False,
                              skip_group_check=True)
                    mm = pe.matmul(o[:, P:TP], vgn[:, 1, v], am[:, h, TP:3 * P], start=False, stop=True,
                                   skip_group_check=True)
                mm.then_inc(done, 1)

            def kd_nat(half):
                out, done = fill("kd_nat", half)
                pe.wait_ge(kd_new, 1)
                for h in range(H_GLA):
                    mm = pe.transpose(out[:, h * P:(h + 1) * P], qe[:, h, half * P:(half + 1) * P],
                                      ident[:, :])
                mm.then_inc(done, 1)

            def state_(pair):
                out, done = fill("state", pair)
                taken(pe, "kd_nat", 0)
                taken(pe, "kd_nat", 1)
                for i in range(2):
                    h = 2 * pair + i
                    for half in range(2):
                        mm = pe.matmul(out[:, i * DV:(i + 1) * DV], kdn[:, half, h * DK:(h + 1) * DK],
                                       vgn[:, half, h * DV:(h + 1) * DV], start=half == 0, stop=half == 1,
                                       skip_group_check=True)
                mm.then_inc(done, 1)

            def rec_out(b):
                out, done = fill("rec_out", b)
                pe.wait_ge(st_new, b + 1)
                for h in range(H_GLA):
                    for t in range(2):
                        mm = pe.matmul(out[:, 2 * h + t:2 * h + t + 1],
                                       stream[:, b % 4, h * DV + t * P:h * DV + (t + 1) * P],
                                       proj["qg"][:, h, TP + b:TP + b + 1], start=True, stop=True,
                                       skip_group_check=True)
                mm.then_inc(done, 1)

            def score(h):
                out, done = fill("score", h)
                m = max(i for i, (_, b, t) in enumerate(BLOCKS) if (b, t) == ("ka", 4 * (h // 8)))
                pe.wait_ge(proj_new, TILES_BEFORE["in", m] + CN_T)
                r = slice(HD * (h % 2), HD * (h % 2) + HD)
                q, k = proj["qa"][r, h // 2, :], proj["ka"][r, h // 2, :]
                pe.matmul(out[:, 0:P], q[:, 0:P], k[:, 0:P], start=True, stop=True, skip_group_check=True)
                pe.matmul(out[:, P:3 * P], q[:, P:TP], k[:, 0:TP], start=True, stop=True,
                          skip_group_check=True).then_inc(done, 1)

            def probs_t(h):
                out, done = fill("probs_t", h)
                pe.wait_ge(p_new, h + 1)
                for i in range(3):
                    mm = pe.transpose(out[:, i * P:(i + 1) * P], sm[:, i * P:(i + 1) * P], ident[:, :])
                mm.then_inc(done, 1)

            def values(h):
                bank, done = fill("values", h)
                taken(pe, "probs_t", h)
                for half in range(2):
                    taken(pe, "nat", ("va", half, h // 8))
                out = bank[HD * (h % 2):HD * (h % 2) + HD, :]
                v = slice(h * HD, (h + 1) * HD)
                pe.matmul(out[:, 0:TP], van[:, 0, v], pt[:, 0:TP], start=True, stop=False,
                          skip_group_check=True)
                pe.matmul(out[:, P:TP], van[:, 1, v], pt[:, TP:3 * P], start=False, stop=True,
                          skip_group_check=True).then_inc(done, 1)

            def s_scores(_):
                out, done = fill("s_scores", 0)
                pe.wait_ge(sc_new, 2 * TS)
                pe.wait_ge(self_new, 1)
                for t in range(2):
                    pe.transpose(out[:, t * P:(t + 1) * P], sc_s[:, t, :, :].rearrange("p h b -> p (h b)"),
                                 ident[:, :])
                pe.matmul(out[:, TP:TP + 1], prod[:, 0:P], ones[:, 0, :], start=True, stop=True,
                          skip_group_check=True).then_inc(done, 1)

            def s_probs(_):
                out, done = fill("s_probs", 0)
                pe.wait_ge(sp_new, 1)
                for t in range(2):
                    pe.transpose(out[:, t * P:(t + 1) * P], sm_s[:, t * P:(t + 1) * P], ident[:, :])
                pe.matmul(out[:, TP:TP + P], ones[:, 0, :].to_broadcast([P, P]), prod[:, 128:256],
                          start=True, stop=True, skip_group_check=True).then_inc(done, 1)

            held = {}

            def s_values(_):
                bank, held["done"] = fill("s_values", 0)
                held["out"] = bank[:, 0:AT_T * 2 * TS].rearrange("p (f e b) -> p f e b", f=AT_T, e=2)
                taken(pe, "s_probs", 0)

            def s_value(b):
                for t in range(2):
                    pe.wait_ge(kc_in[(2 * b + t) % 4], cache_count(b, t, True))
                for f in range(AT_T):
                    for t in range(2):
                        mm = pe.matmul(held["out"][:, f, :, b], stream[:, (2 * b + t) % 4, f * P:(f + 1) * P],
                                       pt_s[:, t, 2 * f:2 * f + 2, b], start=t == 0, stop=t == 1,
                                       skip_group_check=True)
                if b < TS - 1:
                    mm.then_inc(v_used, 1)
                else:
                    mm.then_inc(held["done"], 1)

            def mean_att(_):
                out, done = fill("mean_att", 0)
                pe.wait_ge(asq_new, AT_T + 1)
                pe.matmul(out[:, 0:T], ones[:, 2, :].to_broadcast([P, P]), root[:, :], start=True,
                          stop=True).then_inc(done, 1)

            def gla_mean(h):
                out, done = fill("gla_mean", h)
                pe.wait_ge(gss_new, h + 1)
                pe.matmul(out[:, 0:T], ones[:, 3, :].to_broadcast([P, P]), sqg[:, h, :], start=True,
                          stop=True).then_inc(done, 1)

            def mix_mean(_):
                _, done = fill("mean", "mix")
                mean(2, done)

            for n, (kind, m, j, last) in enumerate(CHUNKS):
                c = MIX + n
                if kind == "lr":
                    if j == 0:
                        lr_out, lr_done = fill("lowrank", 0)
                    pe.wait_ge(lo_done, c + (RING + 1))
                    for t in range(KT // 2):
                        kt = KT // 2 * j + t
                        hi = wh[:, c % RING, :, :].rearrange("p a b -> p (a b)")[:, t * P:(t + 1) * P]
                        lo = wl[:, c % RING, :, :].rearrange("p a b -> p (a b)")[:, t * P:(t + 1) * P]
                        pe.matmul(lr_out[:, 0:T], hi, xh[:, kt, :], start=kt == 0, stop=False)
                        pe.matmul(lr_out[:, 0:T], hi, xl[:, kt, :], start=False, stop=False)
                        mm = pe.matmul(lr_out[:, 0:T], lo, xh[:, kt, :], start=False, stop=kt == KT - 1)
                    mm.then_inc(used, 1)
                    if j == 1:
                        pe.wait_ge(used, c + 1 + RING)
                        pe.sem_inc(lr_done, 1)
                else:
                    before_n = TILES_BEFORE[kind, m]

                    def bank_read(t, b=before_n):
                        if b:
                            pe.wait_ge(proj_new, b - CN_T + t + 1)

                    if n == 0:
                        pe.wait_ge(x_new, 7)
                    if kind == "in":
                        if m == 0 and j % 2 == 0:
                            pe.wait_ge(xl_new, 4 + j // 2 + 1)
                        rhs = lambda t, j=j: (xh[:, CK_T * j + t, :], xl[:, CK_T * j + t, :])
                        first = j == 0
                    elif kind == "gla":
                        pe.wait_ge(og_fin, j // 2 + 1)
                        rhs = lambda t, j=j: (gh[:, CK_T * j + t, :], gl[:, CK_T * j + t, :])
                    else:
                        pe.wait_ge(atl_new, AT_T + 1)
                        rhs = lambda t, j=j: (ath[:, CK_T * j + t, :], atl[:, CK_T * j + t, :])
                    multiply(c, c % RING, rhs, lambda t: g0[:, t, 0:T], j == 0, last,
                             bank_read if j == 0 else None, last)
                for step, arg in PLAN.get(n, ()):
                    if step == "mean":
                        mix_mean(arg)
                    elif step == "nat":
                        nat(*arg)
                    elif step == "gate":
                        gate(arg)
                    elif step == "cum":
                        cumulate(arg)
                    elif step == "level_out":
                        level_out(arg)
                    elif step == "gla_out":
                        gla_out(arg)
                    elif step == "kd_nat":
                        kd_nat(arg)
                    elif step == "state":
                        state_(arg)
                    elif step == "rec_out":
                        rec_out(arg)
                    elif step == "score":
                        score(arg)
                    elif step == "probs_t":
                        probs_t(arg)
                    elif step == "values":
                        values(arg)
                    elif step == "s_scores":
                        s_scores(arg)
                    elif step == "s_probs":
                        s_probs(arg)
                    elif step == "s_values":
                        s_values(arg)
                    elif step == "s_value":
                        s_value(arg)
                    elif step == "mean_att":
                        mean_att(arg)
                    elif step == "gla_mean":
                        gla_mean(arg)

            ffn_in(1, FI2)
            def turn_out(q):
                pe.wait_ge(fin_g, q + 1)
                g = groups[q % 2]
                for half in range(3):
                    rows_n, cols = (P, slice(half * P, (half + 1) * P)) if half < 2 else (TS, slice(TP, T))
                    for n in range(4):
                        mm = pe.transpose(g[0:rows_n, half, n * P:(n + 1) * P], x[:, 4 * q + n, cols],
                                          ident[:, :])
                mm.then_inc(fin_turned, 1)

            for k in range(FO_BLOCKS * FO_CH):
                q, j = k // FO_CH, k % FO_CH
                if j == 0:
                    if q < 2:
                        pe.wait_ge((gate_in, up_in)[q], 2 * FI_BLOCKS)
                    else:
                        pe.wait_ge(fin_rows, q - 1)
                ffn_out_chunk(1, FO2 + k, q, j, (FO2 + k) % RING)
                if j == 6 and q:
                    turn_out(q - 1)
            turn_out(FO_BLOCKS - 1)
            pe.wait_ge(ssq_new, 16)
            for half in range(3):
                n, cols = (P, slice(half * P, (half + 1) * P)) if half < 2 else (TS, slice(TP, T))
                mm = pe.matmul(g0[0:n, 3, half:half + 1], ssq[:, cols], ones[:, 1, :], start=True,
                               stop=True, skip_group_check=True)
            mm.then_inc(fmean_full, 1)

        @block.scalar
        def _(act):
            def split(c, slot, loads, narrow=False):
                act.wait_ge(raw_full[slot], loads * 16)
                act.wait_ge(used, c + 1)
                src, dst = raw[:, slot, :, :], wh[:, slot, :, :]
                if narrow:
                    src = src.rearrange("p a b -> p (a b)")[:, 0:KT // 2 * RANK].rearrange(
                        "p (a b) -> p a b", b=RANK)
                    dst = dst.rearrange("p a b -> p (a b)").rearrange("p (a b) -> p a b", b=P)[:, :, 0:RANK]
                act.activation(dst, src, ACT.Copy).then_inc(hi_done, 1)

            def split_at(c):
                n = c - MIX
                split(c, c % RING, c // RING + 1, 0 <= n < len(CHUNKS) and CHUNKS[n][0] == "lr")

            def x_high(nth, q, gain, dyn=False):
                act.wait_ge(x_new, nth + 1)
                if dyn:
                    act.sem_inc(misc, 1)
                for n in range(4):
                    a = act.activation(xh[:, bass.ds(4 * q + n, 1), :], x[:, bass.ds(4 * q + n, 1), :], ACT.Copy,
                                       scale=gains[:, gain, bass.ds(4 * q + n, 1)])
                a.then_inc(xh_new, 1)
                act.activation(s_buf[:, :, :], x[:, bass.ds(4 * q, 4), :], ACT.Square).then_inc(sq_new, 1)

            def mean_root():
                return act.activation(root[:, :], g1[:, 0, 0:T], ACT.Sqrt, bias=eps[:, 0:1])

            def ffn_in(nth, c0):
                def body(i, first):
                    for k in range(FI_BODY):
                        c = FI_BODY * i + (c0 + k + 3)
                        split(c, (c0 + k + 3) % RING, FI_BODY // RING * i + ((c0 + k + 3) // RING + 1))
                        if first and k == 7:
                            act.wait_ge(mean_full, 1 + nth)
                            mean_root().then_inc(root_new, 1)
                        if k == 8:
                            act.wait_ge(gate_in, i + (FI_BLOCKS * nth + 1))
                            act.activation(s_buf[:, :, :], s_buf[:, :, :], ACT.Silu).then_inc(gate_silu, 1)
                        if k == FI_BODY - 1:
                            act.wait_ge(u_new, i + (FI_BLOCKS * nth + 1))
                            act.sem_inc(misc, 1)
                            act.activation(uh[:, bass.ds(4 * i, 4), :], t_buf[:, :, :], ACT.Copy).then_inc(uh_new, 1)
                body(0, True)
                with act.Fori(1, FI_BLOCKS) as i:
                    body(i, False)

            act.wait_ge(consts_in, 16 * 8)
            act.wait_ge(eps_set, 1)
            for q in range(KT // 4):
                if q:
                    act.wait_ge(sq_part, q)
                x_high(q, q, 0)
                if q < 3:
                    split_at(q)
            ffn_in(0, FI1)
            act.wait_ge(uh_new, FI_BLOCKS)
            with act.Fori(0, FO_BLOCKS // 2) as i:
                for k in range(2 * FO_CH):
                    c = 2 * FO_CH * i + (FO1 + k + 3)
                    split(c, (FO1 + k + 3) % RING, 2 * FO_CH // RING * i + ((FO1 + k + 3) // RING + 1))
                    if k % FO_CH == FO_CH - 1:
                        b = k // FO_CH
                        x_high(2 * i + (4 + b), 2 * i + b, 1, dyn=True)

            n_k, n_s = [0], [0]

            def nat(name, half, grp):
                bank, done = filled(act, "nat", (name, half, grp))
                turn = USE["nat", (name, half, grp), 0]
                cols = slice(512 * grp, 512 * grp + 512)
                if half < 2 and name in ("vg", "va"):
                    dst = (vgn if name == "vg" else van)[:, half, cols]
                elif half < 2:
                    r = n_k[0] % 2
                    if n_k[0] >= 2:
                        act.wait_ge(rows_out[r], 16 * (n_k[0] // 2))
                    dst = rows[:, r, :]
                else:
                    r = n_s[0] % 2
                    if n_s[0] >= 2:
                        act.wait_ge(rowss_out[r], 16 * (n_s[0] // 2))
                    dst = rows_s[0:TS, r, :]
                act.activation(dst, bank[0:TS if half == 2 else P, 0:512], ACT.Copy).then_inc(done, 1)
                if name == "vg" and half < 2:
                    return
                act.wait_ge(free[turn[0]], turn[1] + 1)
                if half == 2:
                    heads = slice(8 * grp, 8 * grp + 8)
                    out = {"vg": lambda: rows_v[:, cols], "qa": lambda: rows_q[:, cols],
                           "ka": lambda: nk_s[0, :, 0, heads, :].rearrange("b h d -> b (h d)"),
                           "va": lambda: nv_s[0, :, 0, heads, :].rearrange("b h d -> b (h d)")}[name]()
                    act.dma_start(out, dst).then_inc(rowss_out[r], 16)
                    n_s[0] += 1
                else:
                    heads = slice(8 * grp, 8 * grp + 8)
                    out = (nk_p if name == "ka" else nv_p)[0, 0, half * P:(half + 1) * P, heads, :]
                    out = out.rearrange("t h d -> t (h d)")
                    if name == "ka":
                        act.dma_start(out, dst).then_inc(rows_out[r], 16)
                        n_k[0] += 1
                    else:
                        act.dma_start(out, dst).then_inc(van_out, 16)

            def gate(_):
                for half in range(3):
                    bank, _ = filled(act, "gate", 0, half)
                    w = D_GK if half < 2 else H_GLA * TS
                    dst = dif[:, 2 * half:2 * half + 2, :].rearrange("p a b -> p (a b)") if half < 2 else tiny[:, 0:w]
                    act.activation(dst, bank[:, 0:w], ACT.Abs).then_inc(act_own, 1)
                    act.wait_ge(act_own, 2 * half + 1)
                    act.activation(dst, dst, ACT.Exp, scale=-1.0).then_inc(act_own, 1)
                    act.wait_ge(act_own, 2 * half + 2)
                    act.activation(dst, dst, ACT.Ln, bias=1.0).then_inc(gate_l, 1)
                act.wait_ge(free[USE["gate", 0, 2][0]], USE["gate", 0, 2][1] + 1)
                act.activation(a_s[:, :, :].rearrange("p h b -> p (h b)"), tiny[:, 0:H_GLA * TS], ACT.Exp,
                               scale=1.0 / TAU).then_inc(a_exp, 1)

            def cumulate(pair):
                bank, done = filled(act, "cum", pair)
                act.activation(cum[:, 2 * pair:2 * pair + 2, :].rearrange("p a b -> p (a b)"), bank,
                               ACT.Copy).then_inc(done, 1)

            def level_in(n):
                w = LEVELS[n]
                act.wait_ge(dif_new, n + 1)
                d = dif[:, :, :].rearrange("p h (b s w) -> p (h b) s w", s=2, w=w)
                act.activation(d[:, :, 0, :], d[:, :, 0, :], ACT.Exp, scale=-1.0)
                act.activation(d[:, :, 1, :], d[:, :, 1, :], ACT.Exp).then_inc(dec_new, 1)

            def level_out(n):
                if n == 0:
                    act.wait_ge(cleared, 5)
                    for pair in range(2):
                        bank, done = filled(act, "level_out", 0, pair)
                        act.activation(am[:, 2 * pair:2 * pair + 2, P:TP],
                                       bank[:, 0:2 * P].rearrange("p (h t) -> p h t", h=2),
                                       ACT.Copy).then_inc(done, 1)

            def gla_out(h):
                bank, done = filled(act, "gla_out", h)
                for g in range(2):
                    taken(act, "nat", ("vg", 2, g))
                act.activation(og[:, 2 * h:2 * h + 2, 0:TP], bank.rearrange("p (a t) -> p a t", a=2),
                               ACT.Copy).then_inc(done, 1)

            def kdecay(_):
                act.wait_ge(dif_new, len(LEVELS) + 1)
                act.activation(dif[:, :, :], dif[:, :, :], ACT.Exp, scale=-1.0).then_inc(dec_new, 1)

            def kd_nat(half):
                bank, done = filled(act, "kd_nat", half)
                act.activation(kdn[:, half, :], bank, ACT.Copy).then_inc(done, 1)

            def state_(pair):
                bank, done = filled(act, "state", pair)
                act.wait_ge(kd_new, 1)
                act.activation(sfin[:, 2 * pair:2 * pair + 2, :].rearrange("p a b -> p (a b)"), bank,
                               ACT.Copy).then_inc(done, 1)

            def rec_out(b):
                bank, done = filled(act, "rec_out", b)
                act.activation(og[:, :, TP + b], bank[:, 0:2 * H_GLA], ACT.Copy).then_inc(done, 1)

            def score(h):
                act.wait_ge(masked, h + 1)
                act.activation(sm[:, 0:P], sm[:, 0:P], ACT.Exp, scale=HD ** -0.5, bias=tiny[:, 2:3])
                act.activation(sm[:, P:3 * P], sm[:, P:3 * P], ACT.Exp, scale=HD ** -0.5,
                               bias=tiny[:, 3:4]).then_inc(e_new, 1)

            def probs_t(h):
                bank, done = filled(act, "probs_t", h)
                if h:
                    bank_v, k = USE["values", h - 1, 0]
                    act.wait_ge(full[bank_v], k + 1)
                act.activation(pt[:, :], bank[:, 0:3 * P], ACT.Copy).then_inc(done, 1)

            def values(h):
                bank, done = filled(act, "values", h)
                r = slice(HD * (h % 2), HD * (h % 2) + HD)
                act.activation(proj["qa"][r, h // 2, 0:TP], bank[r, 0:TP], ACT.Copy).then_inc(done, 1)

            def att_split(f):
                taken(act, "values", 2 * f + 1)
                if f:
                    act.wait_ge(asq_new, f)
                act.activation(ath[:, f, 0:TP], proj["qa"][:, f, 0:TP], ACT.Copy, scale=gatt[:, f:f + 1])
                act.activation(asq[:, 0:TP], proj["qa"][:, f, 0:TP], ACT.Square).then_inc(ath_new, 1)

            def s_scores(_):
                bank, done = filled(act, "s_scores", 0)
                act.wait_ge(smax_new, 1)
                act.activation(sm_s[:, :], bank[:, 0:TP + 1], ACT.Exp, scale=HD ** -0.5,
                               bias=tiny[:, 9:10]).then_inc(done, 1)

            def s_probs(_):
                bank, done = filled(act, "s_probs", 0)
                act.activation(pt_s[:, :, :, :].rearrange("p t h b -> p (t h b)"), bank[:, 0:TP], ACT.Copy)
                act.activation(prod[:, 256:384], bank[:, TP:TP + P], ACT.Copy).then_inc(done, 1)

            def att_split_s(_):
                act.wait_ge(oatts_new, 1)
                act.wait_ge(asq_new, AT_T)
                for f in range(AT_T):
                    act.activation(ath[:, f, TP:T], proj["qa"][:, f, TP:T], ACT.Copy, scale=gatt[:, f:f + 1])
                act.activation(tiny[:, 0:64].rearrange("p (f b) -> p f b", b=TS), proj["qa"][:, :, TP:T],
                               ACT.Square).then_inc(ath_new, 1)

            def mean_att(_):
                bank, done = filled(act, "mean_att", 0)
                act.activation(asq[:, :], bank[:, 0:T], ACT.Sqrt, bias=eps[:, 0:1]).then_inc(done, 1)

            def gla_sq(h):
                if h == 0:
                    taken(act, "rec_out", TS - 1)
                if h >= 2:
                    act.wait_ge(gss_new, h - 1)
                act.activation(rstdg[:, 2 * (h % 2):2 * (h % 2) + 2, :], og[:, 2 * h:2 * h + 2, :],
                               ACT.Square).then_inc(gsq_new, 1)

            def gla_mean(h):
                bank, done = filled(act, "gla_mean", h)
                act.wait_ge(gss_new, H_GLA)
                act.activation(rstdg[:, h, :], bank[:, 0:T], ACT.Sqrt, bias=eps[:, 0:1]).then_inc(done, 1)

            def gla_gate(g):
                act.wait_ge(proj_new, TILES_BEFORE["in", len(BLOCKS) - 2 + g] + CN_T)
                act.activation(rg[:, 4 * g:4 * g + 4, :], rg[:, 4 * g:4 * g + 4, :], ACT.Silu).then_inc(rg_silu, 1)

            def gla_split(g):
                act.wait_ge(og_new, g + 1)
                for t in range(4):
                    a = act.activation(gh[:, 4 * g + t, :], og[:, 4 * g + t, :], ACT.Copy,
                                       scale=ggla[:, t % 2:t % 2 + 1])
                a.then_inc(gh_new, 1)

            for n, (kind, m, j, last) in enumerate(CHUNKS):
                if n:
                    split_at(MIX + n + 2)
                if kind == "att" and last:
                    if m == 0:
                        for r in range(2):
                            act.wait_ge(rowss_out[r], 64)
                            act.wait_ge(rows_out[r], 32)
                    x_high(8 + m, m, 2)
                for step, arg in PLAN.get(n, ()):
                    if step == "mean":
                        _, done = filled(act, "mean", arg)
                        mean_root().then_inc(done, 1)
                    elif step == "nat":
                        nat(*arg)
                    elif step == "gate":
                        gate(arg)
                    elif step == "cum":
                        cumulate(arg)
                    elif step == "level_in":
                        level_in(arg)
                    elif step == "level_out":
                        level_out(arg)
                    elif step == "gla_out":
                        gla_out(arg)
                    elif step == "kdecay":
                        kdecay(arg)
                    elif step == "kd_nat":
                        kd_nat(arg)
                    elif step == "state":
                        state_(arg)
                    elif step == "rec_out":
                        rec_out(arg)
                    elif step == "score":
                        score(arg)
                    elif step == "probs_t":
                        probs_t(arg)
                    elif step == "values":
                        values(arg)
                    elif step == "att_split":
                        att_split(arg)
                    elif step == "s_scores":
                        s_scores(arg)
                    elif step == "s_probs":
                        s_probs(arg)
                    elif step == "att_split_s":
                        att_split_s(arg)
                    elif step == "mean_att":
                        mean_att(arg)
                    elif step == "gla_sq":
                        gla_sq(arg)
                    elif step == "gla_mean":
                        gla_mean(arg)
                    elif step == "gla_gate":
                        gla_gate(arg)
                    elif step == "gla_split":
                        gla_split(arg)

            split_at(FI2 + 2)
            act.wait_ge(rows_out[0], 32)
            act.wait_ge(rows_out[1], 32)
            act.wait_ge(rowss_out[0], 64)
            act.wait_ge(rowss_out[1], 64)
            act.wait_ge(van_out, 64)
            act.wait_ge(stored, 1)
            ffn_in(1, FI2)
            def rows_out_(q):
                act.wait_ge(fin_turned, q + 1)
                g = groups[q % 2]
                for half in range(2):
                    act.activation(yn[:, half, 512 * q:512 * q + 512], g[:, half, :], ACT.Copy)
                act.activation(yns[0:TS, 512 * q:512 * q + 512], g[0:TS, 2, :], ACT.Copy).then_inc(fin_rows, 1)

            for k in range(FO_BLOCKS * FO_CH):
                q, j = k // FO_CH, k % FO_CH
                if FO2 + k + 3 < END:
                    split_at(FO2 + k + 3)
                if j == 10 and q:
                    rows_out_(q - 1)
                if j == FO_CH - 1:
                    act.wait_ge(x_new, 13 + q)
                    act.wait_ge(sq_part, 12 + q)
                    act.activation(s_buf[:, :, :], x[:, 4 * q:4 * q + 4, :], ACT.Square).then_inc(sq_new, 1)
            rows_out_(FO_BLOCKS - 1)
            act.wait_ge(fmean_full, 1)
            for half in range(3):
                n = P if half < 2 else TS
                a = act.activation(tiny[0:n, half:half + 1], g0[0:n, 3, half:half + 1], ACT.Sqrt, bias=eps[0:n, 0:1])
            a.then_inc(froot, 1)
            act.wait_ge(frstd, 3)
            act.wait_ge(fin_rows, 4)
            act.activation(yn[:, 1, :], yn[:, 1, :], ACT.Copy, scale=tiny[:, 5:6]).then_inc(y_new, 1)

        @block.vector
        def _(dve):
            def low(c, slot, narrow=False):
                dve.wait_ge(hi_done, c + 1)
                src, h, dst = raw[:, slot, :, :], wh[:, slot, :, :], wl[:, slot, :, :]
                if narrow:
                    src = src.rearrange("p a b -> p (a b)")[:, 0:KT // 2 * RANK].rearrange(
                        "p (a b) -> p a b", b=RANK)
                    h, dst = (v.rearrange("p a b -> p (a b)").rearrange("p (a b) -> p a b", b=P)[:, :, 0:RANK]
                              for v in (h, dst))
                dve.tensor_tensor(dst, src, h.bitcast(F32), ALU.subtract).then_inc(lo_done, 1)

            def low_at(c):
                n = c - MIX
                low(c, c % RING, 0 <= n < len(CHUNKS) and CHUNKS[n][0] == "lr")

            links = [0]

            def link(ins):
                links[0] += 1
                ins.then_inc(vec, 1)
                dve.wait_ge(vec, links[0])

            def update(q, grp, c_end):
                dve.wait_ge(used, c_end + (1 + RING))
                xq = x[:, bass.ds(4 * q, 4), :]
                dve.scalar_tensor_tensor(out=xq, in0=groups[grp][:, :, 0:T], scalar=0.5, in1=xq,
                                         op0=ALU.mult, op1=ALU.add).then_inc(x_new, 1)

            def add_squares(nth):
                dve.wait_ge(sq_new, nth + 1)
                dve.tensor_reduce(t_buf[:, 0, :], s_buf[:, :, :].rearrange("p k t -> p t k"), AX_X,
                                  ALU.add).then_inc(sq_part, 1)
                dve.wait_ge(sq_part, nth + 1)
                dve.tensor_tensor(ssq[:, :], ssq[:, :], t_buf[:, 0, :], ALU.add).then_inc(ssq_new, 1)

            def x_low(nth, q, gain):
                dve.wait_ge(xh_new, nth + 1)
                for n in range(4):
                    t = bass.ds(4 * q + n, 1)
                    a = dve.scalar_tensor_tensor(out=xl[:, t, :], in0=x[:, t, :], scalar=gains[:, gain, t],
                                                 in1=xh[:, t, :].bitcast(F32), op0=ALU.mult, op1=ALU.subtract)
                a.then_inc(xl_new, 1)
                add_squares(nth)

            def clear_squares():
                link(dve.memset(ssq[:, :], 0.0))

            def factor(nth):
                dve.reciprocal(rstd[:, :], root[:, :]).then_inc(rstd_new, 1)
                dve.wait_ge(rstd_new, nth)

            def wide(v, n=4):
                return v.unsqueeze(1).to_broadcast([P, n, T])

            def ffn_in(nth, c0):
                def body(i, first):
                    for k in range(FI_BODY):
                        low(FI_BODY * i + (c0 + k + 3), (c0 + k + 3) % RING)
                        if k == 7:
                            if first:
                                dve.wait_ge(root_new, 1 + nth)
                                factor(1 + 2 * nth)
                                clear_squares()
                            dve.wait_ge(used, FI_BODY * i + (c0 + FI_BODY // 2 + RING))
                            dve.tensor_tensor(s_buf[:, :, :], g0[:, :, 0:T], wide(rstd[:, :]),
                                              ALU.mult).then_inc(gate_in, 1)
                        if k == FI_BODY - 1:
                            dve.wait_ge(used, FI_BODY * i + (c0 + FI_BODY + RING))
                            if not first:
                                dve.wait_ge(uh_new, i + FI_BLOCKS * nth)
                            dve.tensor_tensor(t_buf[:, :, :], g1[:, :, 0:T], wide(rstd[:, :]),
                                              ALU.mult).then_inc(up_in, 1)
                            dve.wait_ge(up_in, i + (FI_BLOCKS * nth + 1))
                            dve.wait_ge(gate_silu, i + (FI_BLOCKS * nth + 1))
                            dve.tensor_tensor(t_buf[:, :, :], t_buf[:, :, :], s_buf[:, :, :],
                                              ALU.mult).then_inc(u_new, 1)
                            dve.wait_ge(u_new, i + (FI_BLOCKS * nth + 1))
                            dve.wait_ge(uh_new, i + (FI_BLOCKS * nth + 1))
                            dve.tensor_tensor(ul[:, bass.ds(4 * i, 4), :], t_buf[:, :, :],
                                              uh[:, bass.ds(4 * i, 4), :].bitcast(F32),
                                              ALU.subtract).then_inc(ul_new, 1)
                body(0, True)
                with dve.Fori(1, FI_BLOCKS) as i:
                    body(i, False)

            dve.memset(eps[:, :], EPS).then_inc(eps_set, 1)
            dve.sem_inc(lo_done, RING)
            dve.wait_ge(consts_in, 16 * 8)
            clear_squares()
            for q in range(KT // 4):
                dve.wait_ge(x_turned, q + 1)
                dve.tensor_copy(x[:, 4 * q:4 * q + 4, :], groups[q % 2][:, :, 0:T]).then_inc(x_new, 1)
                dve.wait_ge(x_new, q + 1)
                x_low(q, q, 0)
                if q < 3:
                    low_at(q)
            ffn_in(0, FI1)
            with dve.Fori(0, FO_BLOCKS // 2) as i:
                for k in range(2 * FO_CH):
                    low(2 * FO_CH * i + (FO1 + k + 3), (FO1 + k + 3) % RING)
                    if k % FO_CH == FO_CH - 1:
                        b = k // FO_CH
                        update(2 * i + b, b, 2 * FO_CH * i + (FO1 + k))
                        x_low(2 * i + (4 + b), 2 * i + b, 1)

            def take_tiles(n, kind, m, last_c):
                b0 = TILES_BEFORE[kind, m]
                sent = b0 // CN_T * (CN_T - 1)
                for t in range(CN_T):
                    if t < CN_T - 1:
                        dve.wait_ge(tiles, sent + t + 1)
                    else:
                        dve.wait_ge(used, last_c + 1 + RING)
                    src = g0[:, t, 0:T]
                    if kind == "in":
                        _, name, t0 = BLOCKS[m]
                        dst = proj[name][:, t0 + t, :]
                        if name == "qg":
                            a = dve.scalar_tensor_tensor(out=dst, in0=src, scalar=DK ** -0.5, in1=rstd[:, :],
                                                         op0=ALU.mult, op1=ALU.mult)
                        else:
                            a = dve.tensor_tensor(dst, src, rstd[:, :], ALU.mult)
                        a.then_inc(proj_new, 1)
                    elif kind == "gla":
                        xt = x[:, 4 * m + t, :]
                        dve.tensor_tensor(xt, src, xt, ALU.add).then_inc(proj_new, 1)
                    else:
                        tmp = t_buf[:, t, :]
                        dve.tensor_tensor(tmp, src, asq[:, :], ALU.mult).then_inc(proj_new, 1)
                        dve.wait_ge(proj_new, b0 + t + 1)
                        xt = x[:, 4 * m + t, :]
                        a = dve.tensor_tensor(xt, tmp, xt, ALU.add)
                        if t == CN_T - 1:
                            a.then_inc(x_new, 1)

            def lowrank(_):
                bank, done = filled(dve, "lowrank", 0)
                dve.wait_ge(cleared, 5)
                dve.tensor_tensor(lowr[0:RANK, :], bank[0:RANK, 0:T], rstd[0:RANK, :], ALU.mult).then_inc(done, 1)

            def gate(_):
                for half in range(3):
                    bank, done = filled(dve, "gate", 0, half)
                    dve.wait_ge(gate_l, half + 1)
                    w = D_GK if half < 2 else H_GLA * TS
                    l = dif[:, 2 * half:2 * half + 2, :].rearrange("p a b -> p (a b)") if half < 2 else tiny[:, 0:w]
                    dst = la[:, half, :] if half < 2 else tiny[:, 0:w]
                    dve.scalar_tensor_tensor(out=dst, in0=bank[:, 0:w], scalar=0.0, in1=l, op0=ALU.min,
                                             op1=ALU.subtract).then_inc(done, 1)

            def level_in(n):
                w = LEVELS[n]
                if n == 0:
                    taken(dve, "cum", 0)
                    taken(dve, "cum", 1)
                    dve.wait_ge(cleared, 5)
                view = lambda v: v.rearrange("p h (b w) -> p (h b) w", w=2 * w)
                c = view(cum[:, :, :])
                nb = H_GLA * TP // (2 * w)
                dve.tensor_tensor(view(dif[:, :, :]), c, c[:, :, w - 1:w].to_broadcast([P, nb, 2 * w]),
                                  ALU.subtract).then_inc(dif_new, 1)
                if n:
                    bank, k = USE["level_out", n - 1, 1]
                    dve.wait_ge(full[bank], k + 1)
                dve.wait_ge(dec_new, n + 1)
                for dst, src, s in ((ke, "kg", 0), (qe, "qg", 1)):
                    o = dst[:, :, :].rearrange("p h (b s w) -> p h b s w", s=2, w=w)[:, :, :, s, :]
                    i = proj[src][:, :, 0:TP].rearrange("p h (b s w) -> p h b s w", s=2, w=w)[:, :, :, s, :]
                    d = dif[:, :, :].rearrange("p h (b s w) -> p h b s w", s=2, w=w)[:, :, :, s, :]
                    a = dve.tensor_tensor(o, i, d, ALU.mult)
                a.then_inc(qk_new, 1)

            def level_out(n):
                if n == 0:
                    return
                for half in range(2):
                    bank, done = filled(dve, "level_out", n, half)
                    dve.copy_predicated(am[:, :, 2 * P * half:2 * P * half + P],
                                        level[:, n - 1, :].unsqueeze(1).to_broadcast([P, H_GLA, P]),
                                        bank.rearrange("p (h t) -> p h t", h=H_GLA)).then_inc(done, 1)
                    dve.wait_ge(free[USE["level_out", n, half][0]], USE["level_out", n, half][1] + 1)

            def kdecay(_):
                dve.tensor_tensor(dif[:, :, :], cum[:, :, :],
                                  cum[:, :, TP - 1:TP].to_broadcast([P, H_GLA, TP]),
                                  ALU.subtract).then_inc(dif_new, 1)
                bank, k = USE["level_out", len(LEVELS) - 1, 1]
                dve.wait_ge(full[bank], k + 1)
                dve.wait_ge(dec_new, len(LEVELS) + 1)
                dve.tensor_tensor(qe[:, :, :], proj["kg"][:, :, 0:TP], dif[:, :, :], ALU.mult).then_inc(kd_new, 1)

            def rec(b):
                dve.wait_ge(st_in[b % 4], 16 * (b // 4 + 1))
                dve.wait_ge(outer_new, b + 1)
                if b == 0:
                    dve.wait_ge(a_exp, 1)
                for h in range(H_GLA):
                    st = stream[:, b % 4, h * DV:(h + 1) * DV]
                    a = dve.scalar_tensor_tensor(out=st, in0=st, scalar=a_s[:, h, b:b + 1],
                                                 in1=prod[:, h * DV:(h + 1) * DV], op0=ALU.mult, op1=ALU.add)
                a.then_inc(st_new, 1)

            def score(h):
                bank, done = filled(dve, "score", h)
                if h == 0:
                    dve.wait_ge(attc_in, 32)
                    taken(dve, "gate", 0, 2)
                else:
                    b, k = USE["probs_t", h - 1, 0]
                    dve.wait_ge(full[b], k + 1)
                one, two = slice(0, P), slice(P, 3 * P)
                dve.tensor_tensor_reduce(sm[:, one], bank[:, one], mask[:, one], 1.0, NEG, ALU.add, ALU.max,
                                         tiny[:, 0:1])
                k = USE["score", h, 0]
                dve.tensor_tensor_reduce(sm[:, two], bank[:, two], mask[:, two], 1.0, NEG, ALU.add, ALU.max,
                                         tiny[:, 1:2]).then_inc(done, 1)
                dve.wait_ge(free[k[0]], k[1] + 1)
                dve.tensor_scalar(tiny[:, 2:4], tiny[:, 0:2], -HD ** -0.5, None, ALU.mult).then_inc(masked, 1)
                dve.wait_ge(e_new, h + 1)
                dve.tensor_tensor_reduce(sm[:, one], sm[:, one], mult[:, one], 1.0, 0.0, ALU.mult, ALU.add,
                                         tiny[:, 4:5])
                link(dve.tensor_tensor_reduce(sm[:, two], sm[:, two], mult[:, two], 1.0, 0.0, ALU.mult,
                                              ALU.add, tiny[:, 5:6]))
                link(dve.reciprocal(tiny[:, 6:8], tiny[:, 4:6]))
                dve.tensor_scalar(sm[:, one], sm[:, one], tiny[:, 6:7], None, ALU.mult)
                dve.tensor_scalar(sm[:, two], sm[:, two], tiny[:, 7:8], None, ALU.mult).then_inc(p_new, 1)

            def att_split(f):
                dve.wait_ge(ath_new, f + 1)
                if f == 0:
                    link(dve.memset(root[:, :], 0.0))
                dve.scalar_tensor_tensor(out=atl[:, f, 0:TP], in0=proj["qa"][:, f, 0:TP], scalar=gatt[:, f:f + 1],
                                         in1=ath[:, f, 0:TP].bitcast(F32), op0=ALU.mult,
                                         op1=ALU.subtract).then_inc(atl_new, 1)
                if f:
                    dve.wait_ge(asq_new, f)
                dve.tensor_tensor(root[:, 0:TP], root[:, 0:TP], asq[:, 0:TP], ALU.add).then_inc(asq_new, 1)

            def cache_k(b):
                for t in range(2):
                    n = 2 * b + t
                    dve.wait_ge(prod_new, n + 1)
                    dve.tensor_reduce(sc_s[:, t, :, b], stream[:, n % 4, :].rearrange("p (h d) -> p h d", d=HD),
                                      AX_X, ALU.add).then_inc(sc_new, 1)

            def self_score(_):
                taken(dve, "rec_out", TS - 1)
                for name in ("qa", "ka"):
                    m = max(i for i, (_, b, t) in enumerate(BLOCKS) if (b, t) == (name, 4))
                    dve.wait_ge(proj_new, TILES_BEFORE["in", m] + CN_T)
                link(dve.memset(prod[:, 0:P], 0.0))
                for e in range(2):
                    r = slice(HD * e, HD * e + HD)
                    dst = prod[r, 0:P].rearrange("p (f e b) -> p f e b", e=2, b=TS)[:, :, e, :]
                    a = dve.tensor_tensor(dst, proj["qa"][r, :, TP:T], proj["ka"][r, :, TP:T], ALU.mult)
                a.then_inc(self_new, 1)

            def s_scores(_):
                bank, _ = filled(dve, "s_scores", 0)
                link(dve.tensor_reduce(tiny[:, 8:9], bank[:, 0:TP + 1], AX_X, ALU.max))
                dve.tensor_scalar(tiny[:, 9:10], tiny[:, 8:9], -HD ** -0.5, None, ALU.mult).then_inc(smax_new, 1)
                taken(dve, "s_scores", 0)
                dve.wait_ge(sconst_in, 16)
                link(dve.tensor_tensor_reduce(sm_s[:, :], sm_s[:, :], smult[:, :], 1.0, 0.0, ALU.mult, ALU.add,
                                              tiny[:, 10:11]))
                link(dve.reciprocal(tiny[:, 11:12], tiny[:, 10:11]))
                link(dve.tensor_scalar(sm_s[:, :], sm_s[:, :], tiny[:, 11:12], None, ALU.mult))
                dve.tensor_scalar(prod[:, 128:256], ident[:, :], sm_s[:, TP:TP + 1], None,
                                  ALU.mult).then_inc(sp_new, 1)

            def own_value(_):
                bank, done = filled(dve, "s_values", 0)
                taken(dve, "s_probs", 0)
                for e in range(2):
                    r = slice(HD * e, HD * e + HD)
                    own = prod[r, 256:384].rearrange("p (f e b) -> p f e b", e=2, b=TS)[:, :, e, :]
                    tmp = prod[r, 384:448].rearrange("p (f b) -> p f b", b=TS)
                    link(dve.tensor_tensor(tmp, own, proj["va"][r, :, TP:T], ALU.mult))
                    src = bank[r, 0:P].rearrange("p (f e b) -> p f e b", e=2, b=TS)[:, :, e, :]
                    a = dve.tensor_tensor(proj["qa"][r, :, TP:T], src, tmp, ALU.add)
                    if e == 0:
                        link(a)
                    else:
                        a.then_inc(done, 1)
                taken(dve, "s_values", 0)
                dve.sem_inc(oatts_new, 1)

            def att_split_s(_):
                dve.wait_ge(ath_new, AT_T + 1)
                for f in range(AT_T):
                    a = dve.scalar_tensor_tensor(out=atl[:, f, TP:T], in0=proj["qa"][:, f, TP:T],
                                                 scalar=gatt[:, f:f + 1], in1=ath[:, f, TP:T].bitcast(F32),
                                                 op0=ALU.mult, op1=ALU.subtract)
                a.then_inc(atl_new, 1)
                dve.tensor_reduce(root[:, TP:T], tiny[:, 0:64].rearrange("p (f b) -> p b f", b=TS), AX_X,
                                  ALU.add).then_inc(asq_new, 1)

            def mean_att(_):
                taken(dve, "mean_att", 0)
                dve.reciprocal(asq[:, :], asq[:, :]).then_inc(arstd_new, 1)

            def gla_sq(h):
                dve.wait_ge(gsq_new, h + 1)
                dve.tensor_tensor(sqg[:, h, :], rstdg[:, 2 * (h % 2), :], rstdg[:, 2 * (h % 2) + 1, :],
                                  ALU.add).then_inc(gss_new, 1)

            def gla_mean(h):
                taken(dve, "gla_mean", h)
                link(dve.reciprocal(rstdg[:, h, :], rstdg[:, h, :]))
                o = og[:, 2 * h:2 * h + 2, :]
                dve.tensor_tensor(o, o, wide(rstdg[:, h, :], 2), ALU.mult).then_inc(grstd_new, 1)

            def gla_gate(g):
                dve.wait_ge(rg_silu, g + 1)
                dve.wait_ge(grstd_new, H_GLA)
                o = og[:, 4 * g:4 * g + 4, :]
                dve.tensor_tensor(o, o, rg[:, 4 * g:4 * g + 4, :], ALU.mult).then_inc(og_new, 1)

            def gla_split(g):
                dve.wait_ge(og_new, g + 1)
                dve.wait_ge(gh_new, g + 1)
                for t in range(4):
                    k = 4 * g + t
                    a = dve.scalar_tensor_tensor(out=gl[:, k, :], in0=og[:, 4 * g + t, :],
                                                 scalar=ggla[:, t % 2:t % 2 + 1],
                                                 in1=gh[:, k, :].bitcast(F32), op0=ALU.mult, op1=ALU.subtract)
                a.then_inc(og_fin, 1)

            for n, (kind, m, j, last) in enumerate(CHUNKS):
                if n:
                    low_at(MIX + n + 2)
                if last and kind != "lr":
                    if kind == "att" and m == 0:
                        dve.wait_ge(arstd_new, 1)
                        for r in range(2):
                            dve.wait_ge(rowss_out[r], 64)
                            dve.wait_ge(rows_out[r], 32)
                    take_tiles(n, kind, m, MIX + n)
                    if kind == "att":
                        x_low(8 + m, m, 2)
                for step, arg in PLAN.get(n, ()):
                    if step == "mean":
                        taken(dve, "mean", "mix")
                        factor(2)
                        clear_squares()
                    elif step == "lowrank":
                        lowrank(arg)
                    elif step == "gate":
                        gate(arg)
                    elif step == "level_in":
                        level_in(arg)
                    elif step == "level_out":
                        level_out(arg)
                    elif step == "kdecay":
                        kdecay(arg)
                    elif step == "rec":
                        rec(arg)
                    elif step == "score":
                        score(arg)
                    elif step == "att_split":
                        att_split(arg)
                    elif step == "cache_k":
                        cache_k(arg)
                    elif step == "self_score":
                        self_score(arg)
                    elif step == "s_scores":
                        s_scores(arg)
                    elif step == "own_value":
                        own_value(arg)
                    elif step == "att_split_s":
                        att_split_s(arg)
                    elif step == "mean_att":
                        mean_att(arg)
                    elif step == "gla_sq":
                        gla_sq(arg)
                    elif step == "gla_mean":
                        gla_mean(arg)
                    elif step == "gla_gate":
                        gla_gate(arg)
                    elif step == "gla_split":
                        gla_split(arg)

            low_at(FI2 + 2)
            ffn_in(1, FI2)
            for k in range(FO_BLOCKS * FO_CH):
                q, j = k // FO_CH, k % FO_CH
                if FO2 + k + 3 < END:
                    low_at(FO2 + k + 3)
                if j == FO_CH - 1:
                    update(q, q % 2, FO2 + k)
                    add_squares(12 + q)
                    for n in range(4):
                        t = 4 * q + n
                        a = dve.tensor_scalar(x[:, t, :], x[:, t, :], gains[:, 3, t:t + 1], None, ALU.mult)
                    a.then_inc(fin_g, 1)
            dve.wait_ge(froot, 1)
            for half in range(3):
                n = P if half < 2 else TS
                dve.reciprocal(tiny[0:n, 4 + half:5 + half], tiny[0:n, half:half + 1]).then_inc(frstd, 1)
            dve.wait_ge(frstd, 3)
            dve.wait_ge(fin_rows, 4)
            dve.tensor_scalar(yn[:, 0, :], yn[:, 0, :], tiny[:, 4:5], None, ALU.mult).then_inc(y_new, 1)
            dve.tensor_scalar(yns[0:TS, :], yns[0:TS, :], tiny[0:TS, 6:7], None, ALU.mult).then_inc(y_new, 1)

        @block.gpsimd
        def _(pool):
            pool.sem_inc(used, RING)
            pool.dma_start(ident[:, :], c_ident).then_inc(consts_in, 16)
            pool.dma_start(ones[:, :, :], c_ones.rearrange("p (a b) -> p a b", b=1)).then_inc(consts_in, 16)
            with nc.allow_non_contiguous_dma(reason="gains to partitions, a few KB"):
                for n, g in enumerate((g_ffn1[0], g_mix[0], g_ffn2[0], g_final)):
                    pool.dma_start(gains[:, n, :], g.rearrange("(k p) -> p k", p=P)).then_inc(consts_in, 16)
                pool.dma_start(gatt[:, :], g_att[0].rearrange("(k p) -> p k", p=P)).then_inc(consts_in, 16)
                pool.dma_start(ggla[:, :], g_gla[0].rearrange("(k p) -> p k", p=P)).then_inc(consts_in, 16)
            pool.dma_start(smult[:, :], c_smult).then_inc(sconst_in, 16)
            pool.wait_ge(used, MIX + RING)
            pool.dma_start(wg2[0:RANK, :], w_gate2[0]).then_inc(wg2_in, 16)
            pool.dma_start(wg2[RANK:RANK + 1, :], b_gate2).then_inc(wg2_in, 16)
            pool.dma_start(cumw[:, :], c_cum).then_inc(glac_in, 16)
            pool.dma_start(level_f[:, :, :], c_level).then_inc(glac_in, 16)
            pool.memset(lowr[0:32, :], 1.0).then_inc(cleared, 1)
            pool.memset(qe[:, :, :], 0.0).then_inc(cleared, 1)
            pool.memset(ke[:, :, :], 0.0).then_inc(cleared, 1)
            pool.wait_ge(glac_in, 32)
            pool.tensor_copy(level[:, :, :], level_f[:, :, :]).then_inc(cleared, 1)
            pool.wait_ge(cleared, 4)
            pool.memset(am[:, :, :], 0.0).then_inc(cleared, 1)
            for h in range(H_GLA):
                if h % 2 == 0:
                    taken(pool, "state", h // 2)
                pool.dma_start(ns_p[0, 0, h], sfin[:, h, :]).then_inc(sfin_out, 16)
            for h in range(H_GLA):
                taken(pool, "gla_out", h)
            def load_state(b):
                if b >= 4:
                    pool.wait_ge(st_out[b % 4], 16)
                    taken(pool, "rec_out", b - 4)
                pool.dma_start(stream[:, b % 4, :].rearrange("p (h v) -> p h v", h=H_GLA),
                               state[0, b].rearrange("h k v -> k h v")).then_inc(st_in[b % 4], 16)

            for b in range(3):
                load_state(b)
            pool.wait_ge(rowss_out[0], 16)
            pool.wait_ge(rowss_out[1], 16)
            for b in range(TS):
                if b:
                    pool.wait_ge(outer_new, b)
                pool.dma_start(bcast[:, :], rows_v[b:b + 1, :].to_broadcast([P, D_GV])).then_inc(bc_in, 16)
                if b + 3 < TS:
                    load_state(b + 3)
                if b == 0:
                    pool.wait_ge(sfin_out, 64)
                    pool.dma_start(mult[:, :], c_mult).then_inc(attc_in, 16)
                    pool.dma_start(mask[:, :], c_mask).then_inc(attc_in, 16)
                pool.wait_ge(bc_in, 16 * (b + 1))
                if b:
                    pool.wait_ge(st_new, b)
                for h in range(H_GLA):
                    a = pool.tensor_scalar(prod[:, h * DV:(h + 1) * DV], bcast[:, h * DV:(h + 1) * DV],
                                           proj["kg"][:, h, TP + b:TP + b + 1], None, ALU.mult)
                a.then_inc(outer_new, 1)
                pool.wait_ge(st_new, b + 1)
                pool.dma_start(ns_s[0, b].rearrange("h k v -> k h v"),
                               stream[:, b % 4, :].rearrange("p (h v) -> p h v", h=H_GLA)).then_inc(st_out[b % 4], 16)
            def load_cache(cache, b, t):
                rows_of = cache[0, b].rearrange("r h d -> r (h d)")
                slot = (2 * b + t) % 4
                if t == 0:
                    pool.dma_start(stream[:, slot, :], rows_of[PAST - P:PAST, :]).then_inc(kc_in[slot], 16)
                else:
                    pool.dma_start(stream[0:96, slot, :], rows_of[512:896:4, :]).then_inc(kc_in[slot], 16)
                    pool.dma_start(stream[96:128, slot, :], rows_of[0:512:16, :]).then_inc(kc_in[slot], 16)

            for s in range(4):
                pool.wait_ge(st_out[s], 32)
            taken(pool, "rec_out", TS - 1)
            for b in range(2):
                for t in range(2):
                    load_cache(cache_k, b, t)
            for i, (name, g) in enumerate(S_ROWS):
                if name == "qa":
                    pool.wait_ge(rowss_out[i % 2], 16 * (i // 2 + 1))
            for b in range(TS):
                if b:
                    pool.wait_ge(prod_new, 2 * b)
                pool.dma_start(bcast[:, :], rows_q[b:b + 1, :].to_broadcast([P, D_ATT])).then_inc(qb_in, 16)
                pool.wait_ge(qb_in, 16 * (b + 1))
                for t in range(2):
                    slot = (2 * b + t) % 4
                    pool.wait_ge(kc_in[slot], cache_count(b, t, False))
                    pool.tensor_tensor(stream[:, slot, :], stream[:, slot, :], bcast[:, :],
                                       ALU.mult).then_inc(prod_new, 1)
                if b + 2 < TS:
                    for t in range(2):
                        pool.wait_ge(sc_new, 2 * b + t + 1)
                        load_cache(cache_k, b + 2, t)
            for b in range(TS):
                for t in range(2):
                    if b < 2:
                        pool.wait_ge(sc_new, 2 * TS - 4 + 2 * b + t + 1)
                    else:
                        pool.wait_ge(v_used, b - 1)
                    load_cache(cache_v, b, t)
            pool.sem_inc(stored, 1)


_INS = ["x_prompt", "x_sample", "cache_att_k", "cache_att_v", "state_gla", "g_ffn1", "w_ffn1_in",
        "w_ffn1_out", "g_mix", "w_in", "w_gate2", "b_gate2", "g_att_out", "g_gla_out", "w_out", "g_ffn2",
        "w_ffn2_in", "w_ffn2_out", "g_final"]
_OUTS = [(1, TP, D), (TS, 1, D), (1, 1, TP, H_ATT, HD), (1, 1, TP, H_ATT, HD), (1, 1, H_GLA, DK, DV),
         (1, TS, 1, H_ATT, HD), (1, TS, 1, H_ATT, HD), (1, TS, H_GLA, DK, DV)]


def shape_constants():
    import numpy as np
    ident = np.eye(P, dtype=np.float32)
    ones = np.tile(np.array([1, 1 / D, 1 / D_ATT, 1 / DV], np.float32), (P, 1))
    s, t = np.arange(P)[:, None], np.arange(TP)[None, :]
    cum = np.where(s <= t, np.float32(1 / TAU), np.float32(0))
    level = np.zeros((P, len(LEVELS), P), np.float32)
    s, t = np.arange(P)[:, None], np.arange(P)[None, :]
    for n, w in enumerate(LEVELS[1:]):
        level[:, n] = (s // (2 * w) == t // (2 * w)) & (s % (2 * w) < w) & (t % (2 * w) >= w)
    level[:, -1] = s == t
    mult = np.zeros((P, 3 * P), np.float32)
    for i, (qh, kh) in enumerate(((0, 0), (1, 0), (1, 1))):
        dist = (qh - kh) * P + s - t
        for w, d in PATTERNS:
            mult[:, i * P:(i + 1) * P] += (dist >= 0) & (dist <= w) & (dist % d == 0)
    mask = np.where(mult > 0, np.float32(0), np.float32(NEG))
    rows = [*range(PAST - P, PAST), *range(512, PAST - P, 4), *range(0, 512, 16), PAST]
    smult = np.zeros(len(rows), np.float32)
    for w, d in PATTERNS:
        smult += np.array([PAST - r <= w and (PAST - r) % d == 0 for r in rows], np.float32)
    return [ident, ones, cum.astype(np.float32), level, mult, mask, np.tile(smult, (P, 1))]


def kernel(**inputs):
    import numpy as _np
    import concourse.bacc as _bacc
    from concourse import mybir as _mybir
    from concourse.bass_utils import run_bass_kernel_spmd as _run

    nc = _bacc.Bacc("TRN2", target_bir_lowering=False, num_devices=1)
    arrays, args = {}, []
    given = [(name, _np.ascontiguousarray(inputs[name])) for name in _INS]
    given += [(f"const_{i}", a) for i, a in enumerate(shape_constants())]
    for name, a in given:
        arrays[f"in_{name}_dram"] = a
        args.append(nc.dram_tensor(f"in_{name}_dram", a.shape, _mybir.dt.from_np(a.dtype), kind="ExternalInput").ap())
    for i, shape in enumerate(_OUTS):
        args.append(nc.dram_tensor(f"out_{i}_dram", shape, F32, kind="ExternalOutput").ap())
    layer_step(nc, *args)
    r = _run(nc, [arrays], core_ids=[0])
    return tuple(r.results[0][f"out_{i}_dram"] for i in range(len(_OUTS)))
```

```python
from contextlib import ExitStack

import concourse.bass as bass
from concourse import mybir

F32 = mybir.dt.float32
F32R = mybir.dt.float32r
U8 = mybir.dt.uint8
ACT = mybir.ActivationFunctionType
ALU = mybir.AluOpType
AX_X = mybir.AxisListType.X

P = 128
D = 2048
KT = D // P
TP, TS = 256, 8
T = TP + TS
D_FF = 5632
FT = D_FF // P
D_ATT, H_ATT, HD = 1024, 16, 64
AT_T = D_ATT // P
H_GLA, DK, DV = 4, 128, 256
D_GK, D_GV = H_GLA * DK, H_GLA * DV
RANK = 16
TAU = 16.0
EPS = 1e-6
PAST = 1024
PATTERNS = ((128, 1), (512, 4), (2048, 16))
CQ, CK, CV = 0, D_ATT, 2 * D_ATT
CQG = 3 * D_ATT
CKG = CQG + D_GK
CVG = CKG + D_GK
CRG = CVG + D_GV
CLR = CRG + D_GV
NEG = -1.0e38

RING = 4
CK_T, CN_T = 2, 4
CW = CN_T * P
FI_BLOCKS = D_FF // CW
FI_BODY = 2 * KT // CK_T
FO_BLOCKS = D // CW
FO_CH = FT // CK_T
FI1 = 0
FO1 = FI1 + FI_BLOCKS * FI_BODY
MIX = FO1 + FO_BLOCKS * FO_CH

BLOCKS = [(CKG, "kg", 0), ("lr", None, None), (CQG, "qg", 0), (CVG, "vg", 0), (CVG + CW, "vg", 4),
          (CQ, "qa", 0), (CQ + CW, "qa", 4), (CK, "ka", 0), (CV, "va", 0), (CK + CW, "ka", 4),
          (CV + CW, "va", 4), (CRG, "rg", 0), (CRG + CW, "rg", 4)]
IN_CH = KT // CK_T
OUT_CH = IN_CH // 2


def mixer_chunks():
    out = []
    for m, (col, _, _) in enumerate(BLOCKS):
        n = 2 if col == "lr" else IN_CH
        out += [("lr" if col == "lr" else "in", m, j, j == n - 1) for j in range(n)]
    for half in ("gla", "att"):
        for q in range(FO_BLOCKS):
            out += [(half, q, j, j == OUT_CH - 1) for j in range(OUT_CH)]
    return out


CHUNKS = mixer_chunks()
FI2 = MIX + len(CHUNKS)
FO2 = FI2 + FI_BLOCKS * FI_BODY
END = FO2 + FO_BLOCKS * FO_CH
assert (FO_CH * 2) % RING == 0 and FI_BODY % RING == 0


def block_tiles():
    before, n = {}, 0
    for kind, m, j, _ in CHUNKS:
        if j == 0 and kind != "lr":
            before[kind, m] = n
            n += CN_T
    return before, n


TILES_BEFORE, MIX_TILES = block_tiles()


def end_slot(kind, m):
    return max(i for i, (k, b, _, _) in enumerate(CHUNKS) if (k, b) == (kind, m))


SP_AHEAD, SP_LAG = 7, 3
LEVELS = (128, 64, 32, 16, 8, 4, 2, 1)


def mixer_plan():
    plan = {}

    def put(slot, *step):
        plan.setdefault(slot, []).append(step)

    by_buf = {(b, t): end_slot("in", m) for m, (_, b, t) in enumerate(BLOCKS) if b}
    lr = end_slot("lr", 1)
    put(2, "mean", "mix")
    put(lr, "lowrank", 0)
    put(lr + 2, "gate", 0)
    put(lr + 7, "cum", 0)
    put(lr + 8, "cum", 1)
    for g in range(2):
        for part in range(3):
            put(by_buf["vg", 4 * g] + 2 + part, "nat", ("vg", part, g))
    s = by_buf["qg", 0] + 1
    for n in range(len(LEVELS)):
        put(s + 2 * n, "level_dif", n)
        put(s + 2 * n + 1, "level_mul", n)
        if n:
            put(s + 2 * n + 1, "level_add", n - 1)
        put(s + 2 * n + 2, "level_out", n)
    s += 2 * len(LEVELS)
    put(s + 1, "level_add", len(LEVELS) - 1)
    put(s, "kdecay_dif", 0)
    put(s + 1, "kdecay_mul", 0)
    put(s + 1, "level_out", len(LEVELS))
    put(s + 2, "level_add", len(LEVELS))
    s = max(s + 2, by_buf["vg", 4] + 5)
    put(s, "kd_nat", 0)
    put(s + 1, "kd_nat", 1)
    for h in range(H_GLA):
        put(s + 1 + h, "gla_out", h)
    put(s + 4, "state", 0)
    put(s + 5, "state", 1)
    assert s + 7 < by_buf["va", 0]
    s += 9
    for b in range(TS):
        put(s + 2 * b, "rec", b)
        put(s + 2 * b + 2, "rec_out", b)
        put(max(s + 2 * b + SP_LAG, s + SP_LAG) if b < 4 else s + 2 * b + SP_LAG - 1, "load_state", b)
        put(s + 2 * b + SP_LAG, "load_v_row", b)
    rec_end = s + 2 + 2 * (TS - 1)
    for grp in range(2):
        s = by_buf["va", 4 * grp] + 1
        put(s, "nat", ("va", 0, grp))
        put(s + 1, "nat", ("va", 1, grp))
        put(s + 2, "nat", ("ka", 0, grp))
        put(s + 3, "nat", ("ka", 1, grp))
        put(s + 4, "nat", ("va", 2, grp))
        put(s + 5, "nat", ("ka", 2, grp))
        put(by_buf["qa", 4 * grp] + 2, "nat", ("qa", 2, grp))
        for i in range(H_ATT // 2):
            h = H_ATT // 2 * grp + i
            put(s + 2 * i, "score", h)
            put(s + 2 * i + 2, "norm", h)
            put(s + 2 * i + 1, "exp", h)
            put(s + 2 * i + 3, "probs_t", h)
            put(s + 2 * i + 5, "values", h)
            if h % 2:
                put(s + 2 * i + 7, "att_split", h // 2)
    s = max(rec_end - 4 + SP_AHEAD, by_buf["qa", 4] + 2 + SP_AHEAD) - SP_LAG + 1
    for b in range(TS):
        put(s + 3 * b, "cache_k", b)
        put(s + 3 * b + SP_LAG, "load_k", b)
    s += 3 * TS - 2
    put(s, "self_score", 0)
    put(s + 1, "s_scores", 0)
    put(s + 2, "s_norm", 0)
    put(s + 3, "s_probs", 0)
    s += 8
    put(s, "s_values", 0)
    for b in range(TS):
        put(s + 2 * b, "s_value", b)
        put(s + 2 * b + SP_LAG - 2, "load_v", b)
    s += 2 * TS
    put(s, "own_value", 0)
    put(s + 1, "att_split_s", 0)
    put(s + 2, "mean_att", 0)
    s -= 11
    assert s + 11 < end_slot("gla", FO_BLOCKS - 1), s
    g = by_buf["rg", 0] - 3
    for h in range(H_GLA):
        put(g + h // 2, "gla_sq", h)
        put(g + 2 + 2 * h, "gla_mean", h)
    put(g + 9, "gla_gate", 0)
    put(g + 10, "gla_split", 0)
    put(by_buf["rg", 4], "gla_gate", 1)
    put(by_buf["rg", 4], "gla_split", 1)
    return {k: plan[k] for k in sorted(plan)}


PLAN = mixer_plan()
S_ROWS = [arg[::2] for steps in PLAN.values() for step, arg in steps if step == "nat" and arg[1] == 2]
BANKS = {"mean": (0,), "lowrank": (1,), "gate": (0, 1, 2), "cum": (0,), "nat": (3,),
         "level_out": (1, 2), "gla_out": (0,), "kd_nat": (3,), "state": (1,), "rec_out": (3,),
         "score": (0,), "probs_t": (1,), "values": (2,), "s_scores": (3,),
         "s_probs": (3,), "s_values": (3,), "mean_att": (0,), "gla_mean": (2,)}


def cache_count(b, t, is_value):
    return 16 * (1 + t) * ((TS // 2 if is_value else 0) + b // 2 + 1)


def uses_of_banks():
    uses, count = {}, [0] * 4
    for steps in PLAN.values():
        for step, arg in steps:
            for n, bank in enumerate(BANKS.get(step, ())):
                uses[step, arg, n] = (bank, count[bank])
                count[bank] += 1
    return uses, count


USE, USES = uses_of_banks()


def layer_step(nc, x_prompt, x_sample, cache_k, cache_v, state, g_ffn1, w1_in, w1_out, g_mix, w_in,
               w_gate2, b_gate2, g_att, g_gla, w_out, g_ffn2, w2_in, w2_out, g_final,
               c_ident, c_ones, c_cum, c_level, c_mult, c_mask, c_smult,
               y_p, y_s, nk_p, nv_p, ns_p, nk_s, nv_s, ns_s):
    rows_q = nc.dram_tensor("rows_q", (TS, D_ATT), F32, kind="Internal").ap()
    rows_v = nc.dram_tensor("rows_v", (TS, D_GV), F32, kind="Internal").ap()
    with ExitStack() as ctx:
        base = (nc.sbuf_base + 63) // 64 * 64
        ctx.enter_context(nc.sbuf_tensor("arena", [P, (212800 - 64) // 4], F32))

        def at(name, offset, shape, dt=F32):
            return nc.alloc_sbuf_tensor_at(name, [P, *shape], dt, offset=base + offset)

        here = [0]

        def sb(name, shape, dt=F32):
            size = 1 if dt == U8 else 4
            for n in shape:
                size *= n
            t = at(name, here[0], shape, dt)
            here[0] += (size + 31) // 32 * 32
            return t

        x = sb("x", [KT, T])
        xh, xl = sb("xh", [KT, T], F32R), sb("xl", [KT, T], F32R)
        raw = sb("raw", [RING, CK_T, CW])
        wh, wl = sb("wh", [RING, CK_T, CW], F32R), sb("wl", [RING, CK_T, CW], F32R)
        ident = sb("ident", [P])
        ones = sb("ones", [4, 1])
        eps = sb("eps", [1])
        ssq = sb("ssq", [T])
        rstd = sb("rstd", [T])
        asq = sb("asq", [T])
        root = sb("root", [T])
        all_gains = sb("all_gains", [4 * KT + AT_T + DV // P])
        gains = all_gains[:, 0:4 * KT].rearrange("p (n k) -> p n k", k=KT)
        gatt = all_gains[:, 4 * KT:4 * KT + AT_T]
        ggla = all_gains[:, 4 * KT + AT_T:]
        sc_s = sb("sc_s", [2, H_ATT, TS])
        sm_s = sb("sm_s", [257])
        smult = sb("smult", [257])
        pt_s = sb("pt_s", [2, H_ATT, TS])
        tiny = sb("tiny", [64])
        a_s = sb("a_s", [H_GLA, TS])
        s_start = here[0]
        s_buf = sb("s_buf", [4, T])
        t_buf = sb("t_buf", [4, T])
        u_at = here[0]
        uh, ul = sb("uh", [FT, T], F32R), sb("ul", [FT, T], F32R)
        assert here[0] <= 212800 - 64, here[0]
        xn = at("xn", u_at, [2, D])
        xns = at("xns", u_at + 2 * D * 4, [D])
        gain_rows = at("gain_rows", u_at + 3 * D * 4, [P])
        here[0] = u_at
        proj = {name: sb(name, [n, T]) for name, n in
                (("qa", AT_T), ("ka", AT_T), ("va", AT_T), ("qg", H_GLA), ("kg", H_GLA), ("vg", AT_T),
                 ("rg", AT_T))}
        og = proj["vg"]
        rg = proj["rg"]
        lowr = sb("lowr", [T])
        wg2 = sb("wg2", [D_GK])
        work = here[0]
        la = sb("la", [2, D_GK])
        cum = sb("cum", [H_GLA, TP])
        dif = sb("dif", [H_GLA, TP])
        qe, ke = sb("qe", [H_GLA, TP]), sb("ke", [H_GLA, TP])
        am = sb("am", [H_GLA, 3 * P])
        vgn = sb("vgn", [2, D_GV])
        cumw = sb("cumw", [TP])
        level = sb("level", [len(LEVELS), P], U8)
        assert here[0] <= u_at + 2 * FT * T * 4
        level_f = at("level_f", work + 5 * 4096, [len(LEVELS), P])
        kdn = at("kdn", work, [2, D_GK])
        sfin = at("sfin", work + 2 * 4096, [H_GLA, DV])
        here[0] = work
        van = sb("van", [2, D_ATT])
        sm = sb("sm", [2, 3 * P])
        pt = sb("pt", [3 * P])
        mult, mask = sb("mult", [3 * P]), sb("mask", [3 * P])
        stream = sb("stream", [4, 1024])
        bcast = sb("bcast", [2, 1024])
        assert here[0] <= 212800 - 64
        prod = at("prod", u_at + (4 * AT_T + 2 * H_GLA + AT_T) * T * 4, [448])
        rows = at("rows", s_start, [2, 512])
        rows_s = at("rows_s", s_start + 4096, [2, 512])
        sqg = at("sqg", u_at + 3 * AT_T * T * 4, [H_GLA, T])
        rstdg = at("rstdg", u_at + (3 * AT_T + H_GLA) * T * 4, [H_GLA, T])
        gh = at("gh", u_at + 3 * AT_T * T * 4, [AT_T, T], F32R)
        gl = at("gl", u_at + (4 * AT_T + 2 * H_GLA) * T * 4, [AT_T, T], F32R)
        ath = at("ath", u_at + AT_T * T * 4, [AT_T, T], F32R)
        atl = at("atl", u_at + 2 * AT_T * T * 4, [AT_T, T], F32R)
        yn = at("yn", KT * T * 4, [2, D])
        yns = at("yns", KT * T * 4 + 2 * D * 4, [D])

        g0 = ctx.enter_context(nc.psum_tensor("g0", [P, 4, 512], F32))
        g1 = ctx.enter_context(nc.psum_tensor("g1", [P, 4, 512], F32))
        groups = (g0, g1)

        def sem(name):
            return ctx.enter_context(nc.semaphore(name))

        def sems(name, n):
            return [sem(f"{name}{i}") for i in range(n)]

        raw_full = sems("raw_full", RING)
        hi_done = sem("hi_done")
        lo_done = sem("lo_done")
        used = sem("used")
        ident_in, consts_in, sconst_in = sem("ident_in"), sem("consts_in"), sem("sconst_in")
        gains_in, gains_full, gains_new = sem("gains_in"), sem("gains_full"), sem("gains_new")
        glac_in, attc_in, wg2_in = sem("glac_in"), sem("attc_in"), sem("wg2_in")
        eps_set, cleared = sem("eps_set"), sem("cleared")
        x_in, xs_in = sems("x_in", KT // 4), sem("xs_in")
        x_turned = sem("x_turned")
        x_even, x_odd = sem("x_even"), sem("x_odd")
        x_new = sem("x_new")
        xh_new, xl_new = sem("xh_new"), sem("xl_new")
        sq_new, sq_part, ssq_new = sem("sq_new"), sem("sq_part"), sem("ssq_new")
        mean_full, root_new, rstd_new = sem("mean_full"), sem("root_new"), sem("rstd_new")
        gate_in, gate_silu = sem("gate_in"), sem("gate_silu")
        up_in, u_new = sem("up_in"), sem("u_new")
        uh_new, ul_new = sem("uh_new"), sem("ul_new")
        tiles = sem("tiles")
        proj_new = sem("proj_new")
        full = sems("bank_full", 4)
        free = sems("bank_free", 4)
        vec, act_own = sem("vec"), sem("act_own")
        misc = sem("misc")
        gate_l, a_exp = sem("gate_l"), sem("a_exp")
        dif_new, dec_new = sem("dif_new"), sem("dec_new")
        qk_new, kd_new = sem("qk_new"), sem("kd_new")
        sfin_out = sem("sfin_out")
        gsq_new, gss_new, grstd_new = sem("gsq_new"), sem("gss_new"), sem("grstd_new")
        rg_silu, og_new, gh_new, og_fin = sem("rg_silu"), sem("og_new"), sem("gh_new"), sem("og_fin")
        rows_out, rowss_out, van_out = sems("rows_out", 2), sems("rowss_out", 2), sem("van_out")
        st_in, st_out, kc_in = sems("st_in", 4), sems("st_out", 4), sems("kc_in", 4)
        bc_in = sems("bc_in", 2)
        decayed, st_new = sem("decayed"), sem("st_new")
        prod_new, sc_new, self_new = sem("prod_new"), sem("sc_new"), sem("self_new")
        smax_new, sp_new = sem("smax_new"), sem("sp_new")
        weighted, v_used = sem("weighted"), sem("v_used")
        oatts_new = sem("oatts_new")
        masked, e_new, p_new = sem("masked"), sem("e_new"), sem("p_new")
        ath_new, atl_new = sem("ath_new"), sem("atl_new")
        asq_new, arstd_new = sem("asq_new"), sem("arstd_new")
        stored = sem("stored")
        fin_g, fin_turned, fin_rows = sem("fin_g"), sem("fin_turned"), sem("fin_rows")
        fmean_full, froot, frstd = sem("fmean_full"), sem("froot"), sem("frstd")
        y_new, y_out = sem("y_new"), sem("y_out")

        def taken(eng, step, arg, n=0):
            bank, k = USE[step, arg, n]
            eng.wait_ge(free[bank], k + 1)

        def filled(eng, step, arg, n=0):
            bank, k = USE[step, arg, n]
            eng.wait_ge(full[bank], k + 1)
            return g1[:, bank, :], free[bank]

        block = ctx.enter_context(nc.Block())

        @block.sync
        def _(sp):
            def load(c, slot, src, shape=None):
                sp.wait_ge(lo_done, c + 1)
                dst = raw[:, slot, :, :]
                if shape:
                    dst = dst.rearrange("p a b -> p (a b)")[:, 0:shape[0] * shape[1]].rearrange(
                        "p (a b) -> p a b", a=shape[0])
                sp.dma_start(dst, src).then_inc(raw_full[slot], 16)

            def rows_of(w, k, n, cols):
                return w[k * P:(k + n) * P, cols].rearrange("(t p) n -> p t n", p=P)

            def ffn_in(w, c0, loaded=0):
                def body(i, k0):
                    for k in range(k0, FI_BODY):
                        j, up = k % (FI_BODY // 2), k // (FI_BODY // 2)
                        load(FI_BODY * i + (c0 + k), (c0 + k) % RING,
                             rows_of(w, CK_T * j, CK_T, bass.ds(CW * i + up * D_FF, CW)))
                body(0, loaded)
                with sp.Fori(1, FI_BLOCKS) as i:
                    body(i, 0)

            def ffn_out_pairs(w, c0):
                with sp.Fori(0, FO_BLOCKS // 2) as i:
                    for k in range(2 * FO_CH):
                        b, j = k // FO_CH, k % FO_CH
                        load(2 * FO_CH * i + (c0 + k), (c0 + k) % RING,
                             rows_of(w, CK_T * j, CK_T, bass.ds(2 * CW * i + b * CW, CW)))

            def load_x(q):
                cols = slice(q * CW, (q + 1) * CW)
                src = x_prompt[0, :, cols].rearrange("(h p) d -> p h d", p=P)
                sp.dma_start(xn[:, :, cols], src).then_inc(x_in[q], 16)

            def load_first(c):
                load(FI1 + c, (FI1 + c) % RING, rows_of(w1_in[0], CK_T * c, CK_T, slice(0, CW)))

            load_x(0)
            sp.dma_start(xns[0:TS, :], x_sample[:, 0, :]).then_inc(xs_in, 16)
            load_x(1)
            sp.wait_ge(gains_in, 16 * 6)
            load_first(0)
            load_x(2)
            load_first(1)
            load_x(3)
            load_first(2)
            load_first(3)
            ffn_in(w1_in[0], FI1, loaded=4)
            ffn_out_pairs(w1_out[0], FO1)

            def load_state(b):
                if b < 4:
                    taken(sp, "state", 1)
                    taken(sp, "gla_out", H_GLA - 1)
                    taken(sp, "level_out", len(LEVELS), 1)
                else:
                    sp.wait_ge(st_out[b % 4], 16)
                    taken(sp, "rec_out", b - 4)
                sp.dma_start(stream[:, b % 4, :].rearrange("p (h v) -> p h v", h=H_GLA),
                             state[0, b].rearrange("h k v -> k h v")).then_inc(st_in[b % 4], 16)

            def load_v_row(b):
                if b < 2:
                    sp.wait_ge(rowss_out[b], 16)
                    sp.wait_ge(rowss_out[1 - b], 16)
                else:
                    sp.wait_ge(st_new, b - 1)
                sp.dma_start(bcast[:, b % 2, :], rows_v[b:b + 1, :].to_broadcast([P, D_GV])).then_inc(bc_in[b % 2], 16)

            def load_cache(cache, b):
                rows_of = cache[0, b].rearrange("r h d -> r (h d)")
                one, two = (2 * b) % 4, (2 * b + 1) % 4
                sp.dma_start(stream[:, one, :], rows_of[PAST - P:PAST, :]).then_inc(kc_in[one], 16)
                sp.dma_start(stream[0:96, two, :], rows_of[512:896:4, :]).then_inc(kc_in[two], 16)
                sp.dma_start(stream[96:128, two, :], rows_of[0:512:16, :]).then_inc(kc_in[two], 16)

            def load_k(b):
                if b < 2:
                    for t in range(2):
                        sp.wait_ge(st_out[2 * b + t], 32)
                        taken(sp, "rec_out", 4 + 2 * b + t)
                    sp.wait_ge(st_new, TS - 1 + b)
                    for i, (name, _) in enumerate(S_ROWS):
                        if name == "qa":
                            sp.wait_ge(rowss_out[i % 2], 16 * (i // 2 + 1))
                else:
                    sp.wait_ge(sc_new, 2 * (b - 1))
                load_cache(cache_k, b)
                if b >= 2:
                    sp.wait_ge(prod_new, 2 * (b - 1))
                sp.dma_start(bcast[:, b % 2, :], rows_q[b:b + 1, :].to_broadcast([P, D_ATT])).then_inc(bc_in[b % 2], 16)

            def load_v(b):
                if b < 2:
                    sp.wait_ge(sc_new, 2 * TS - 2 + 2 * b)
                else:
                    sp.wait_ge(v_used, b - 1)
                load_cache(cache_v, b)

            for n, (kind, m, j, _) in enumerate(CHUNKS):
                c = MIX + n
                if kind == "in":
                    src = rows_of(w_in[0], CK_T * j, CK_T, slice(BLOCKS[m][0], BLOCKS[m][0] + CW))
                    load(c, c % RING, src)
                elif kind == "lr":
                    load(c, c % RING, rows_of(w_in[0], KT // 2 * j, KT // 2, slice(CLR, CLR + RANK)),
                         (KT // 2, RANK))
                else:
                    k0 = (AT_T if kind == "gla" else 0) + CK_T * j
                    load(c, c % RING, rows_of(w_out[0], k0, CK_T, slice(m * CW, (m + 1) * CW)))
                for step, arg in PLAN.get(n, ()):
                    if step == "load_state":
                        load_state(arg)
                    elif step == "load_v_row":
                        load_v_row(arg)
                    elif step == "load_k":
                        load_k(arg)
                    elif step == "load_v":
                        load_v(arg)
            ffn_in(w2_in[0], FI2)
            ffn_out_pairs(w2_out[0], FO2)
            for half in range(2):
                sp.wait_ge(y_new, half + 1)
                sp.wait_ge(fin_rows, FO_BLOCKS + half)
                sp.dma_start(y_p[0, half * P:(half + 1) * P, :], yn[:, half, :]).then_inc(y_out, 16)
            sp.wait_ge(y_new, 3)
            sp.wait_ge(fin_rows, FO_BLOCKS + 2)
            sp.dma_start(y_s[:, 0, :], yns[0:TS, :]).then_inc(y_out, 16)
            sp.wait_ge(y_out, 48)

        @block.tensor
        def _(pe):
            def multiply(c, slot, rhs, out, first, last, before=None, tile_sems=False):
                pe.wait_ge(lo_done, c + (RING + 1))
                for n in range(CN_T):
                    if before:
                        before(n)
                    for k in range(CK_T):
                        a, b = rhs(k)
                        hi = wh[:, slot, k, n * P:(n + 1) * P]
                        lo = wl[:, slot, k, n * P:(n + 1) * P]
                        pe.matmul(out(n), hi, a, start=first and k == 0, stop=False)
                        pe.matmul(out(n), hi, b, start=False, stop=False)
                        mm = pe.matmul(out(n), lo, a, start=False, stop=last and k == CK_T - 1)
                    if tile_sems and n < CN_T - 1:
                        mm.then_inc(tiles, 1)
                mm.then_inc(used, 1)

            def mean(nth, done):
                pe.wait_ge(ssq_new, 4 * nth)
                pe.wait_ge(consts_in, 16)
                pe.matmul(g1[:, 0, 0:T], ones[:, 1, :].to_broadcast([P, P]), ssq[:, :], start=True,
                          stop=True).then_inc(done, 1)

            def final_read(n):
                pe.wait_ge(proj_new, MIX_TILES - CN_T + n + 1)

            def ffn_in(nth, c0):
                def body(i, first):
                    for k in range(FI_BODY):
                        j, up = k % (FI_BODY // 2), k // (FI_BODY // 2)
                        if k == 0 and not first:
                            pe.wait_ge(gate_in, i + FI_BLOCKS * nth)
                        if k == 0 and first:
                            if nth == 0:
                                pe.wait_ge(x_even, 2)
                        if first and k == 6:
                            if nth == 0:
                                pe.wait_ge(x_odd, 2)
                            else:
                                for b in range(4):
                                    pe.wait_ge(free[b], USES[b])
                            mean(1 + 2 * nth, mean_full)
                        if k == FI_BODY // 2:
                            if first:
                                pe.wait_ge(root_new, 1 + nth)
                            else:
                                pe.wait_ge(up_in, i + FI_BLOCKS * nth)
                        if first and not up and j % 2 == 0:
                            pe.wait_ge(xl_new, 8 * nth + j // 2 + 1)
                        multiply(FI_BODY * i + (c0 + k), (c0 + k) % RING,
                                 lambda t: (xh[:, CK_T * j + t, :], xl[:, CK_T * j + t, :]),
                                 lambda n: groups[up][:, n, 0:T], j == 0, j == KT // CK_T - 1,
                                 final_read if k == 0 and first and nth else None)
                body(0, True)
                with pe.Fori(1, FI_BLOCKS) as i:
                    body(i, False)

            def ffn_out_chunk(nth, c, q, j, slot):
                if j % 2 == 0:
                    pe.wait_ge(ul_new, FI_BLOCKS * nth + j // 2 + 1)
                multiply(c, slot, lambda t: (uh[:, CK_T * j + t, :], ul[:, CK_T * j + t, :]),
                         lambda n: groups[q % 2][:, n, 0:T], j == 0, j == FO_CH - 1)

            pe.wait_ge(ident_in, 16)
            for q in range(KT // 4):
                if q >= 2:
                    pe.wait_ge((x_even, x_odd)[q % 2], 1)
                if q == 1:
                    pe.wait_ge(gains_in, 16 * 6)
                    n_g = 4 * KT + AT_T + DV // P
                    pe.transpose(g1[:, 3, 0:n_g], gain_rows[0:n_g, :], ident[0:n_g, 0:n_g]).then_inc(gains_full, 1)
                    pe.wait_ge(gains_new, 1)
                pe.wait_ge(x_in[q], 16)
                if q == 0:
                    pe.wait_ge(xs_in, 16)
                for n in range(4):
                    f = slice((4 * q + n) * P, (4 * q + n + 1) * P)
                    g = groups[q % 2]
                    for half in range(2):
                        pe.transpose(g[:, n, half * P:(half + 1) * P], xn[:, half, f], ident[:, :])
                    mm = pe.transpose(g[:, n, TP:T], xns[0:TS, f], ident[0:TS, 0:TS])
                mm.then_inc(x_turned, 1)

            ffn_in(0, FI1)
            with pe.Fori(0, FO_BLOCKS // 2) as i:
                for k in range(2 * FO_CH):
                    b, j = k // FO_CH, k % FO_CH
                    if j == 0:
                        if b == 0:
                            pe.wait_ge(gate_in, FI_BLOCKS)
                            pe.wait_ge(x_new, 2 * i + 3)
                        else:
                            pe.wait_ge(up_in, FI_BLOCKS)
                            pe.wait_ge(x_new, 2 * i + 4)
                    ffn_out_chunk(0, 2 * FO_CH * i + (FO1 + k), b, j, (FO1 + k) % RING)

            def fill(step, arg, n=0):
                bank, k = USE[step, arg, n]
                if k:
                    pe.wait_ge(free[bank], k)
                else:
                    pe.wait_ge(x_new, 8)
                return g1[:, bank, :], full[bank]

            NAT = {"vg": 0, "va": 1, "ka": 2, "qa": 3}

            def nat(name, half, grp):
                out, done = fill("nat", (name, half, grp))
                m = max(i for i, (_, b, t) in enumerate(BLOCKS) if (b, t) == (name, 4 * grp))
                pe.wait_ge(proj_new, TILES_BEFORE["in", m] + CN_T)
                cols, n = (slice(half * P, (half + 1) * P), P) if half < 2 else (slice(TP, T), TS)
                for t in range(4):
                    mm = pe.transpose(out[0:n, t * P:(t + 1) * P], proj[name][:, 4 * grp + t, cols],
                                      ident[:, :])
                mm.then_inc(done, 1)

            def gate(_):
                taken(pe, "lowrank", 0)
                pe.wait_ge(wg2_in, 32)
                for half in range(2):
                    out, done = fill("gate", 0, half)
                    pe.matmul(out[:, 0:D_GK], lowr[0:RANK + 1, half * P:(half + 1) * P],
                              wg2[0:RANK + 1, :], start=True, stop=True).then_inc(done, 1)
                out, done = fill("gate", 0, 2)
                for h in range(H_GLA):
                    mm = pe.matmul(out[:, h * TS:(h + 1) * TS], wg2[0:RANK + 1, h * DK:(h + 1) * DK],
                                   lowr[0:RANK + 1, TP:T], start=True, stop=True)
                mm.then_inc(done, 1)

            def cumulate(pair):
                out, done = fill("cum", pair)
                taken(pe, "gate", 0, 0)
                taken(pe, "gate", 0, 1)
                pe.wait_ge(glac_in, 32)
                for i in range(2):
                    h = slice((2 * pair + i) * DK, (2 * pair + i + 1) * DK)
                    o = out[:, i * TP:(i + 1) * TP]
                    pe.matmul(o, la[:, 0, h], cumw[:, :], start=True, stop=False, skip_group_check=True)
                    mm = pe.matmul(o[:, P:TP], la[:, 1, h], cumw[:, 0:P], start=False, stop=True,
                                   skip_group_check=True)
                mm.then_inc(done, 1)

            def level_out(n):
                if n < len(LEVELS):
                    pe.wait_ge(qk_new, n + 1)
                for half in range(2):
                    out, done = fill("level_out", n, half)
                    tok = slice(half * P, (half + 1) * P)
                    for i in range(2 if n == 0 else H_GLA):
                        if n == 0:
                            h = 2 * half + i
                            k, q = ke[:, h, 0:P], qe[:, h, P:TP]
                        elif n < len(LEVELS):
                            k, q = ke[:, i, tok], qe[:, i, tok]
                        else:
                            k, q = proj["kg"][:, i, tok], proj["qg"][:, i, tok]
                        mm = pe.matmul(out[:, i * P:(i + 1) * P], k, q, start=True, stop=True,
                                       skip_group_check=True)
                    mm.then_inc(done, 1)

            def gla_out(h):
                out, done = fill("gla_out", h)
                for i in range(2):
                    taken(pe, "level_out", 0, i)
                    taken(pe, "level_out", len(LEVELS), i)
                    for g in range(2):
                        taken(pe, "nat", ("vg", i, g))
                for t in range(2):
                    v = slice((2 * h + t) * P, (2 * h + t + 1) * P)
                    o = out[:, t * TP:(t + 1) * TP]
                    pe.matmul(o, vgn[:, 0, v], am[:, h, 0:TP], start=True, stop=False,
                              skip_group_check=True)
                    mm = pe.matmul(o[:, P:TP], vgn[:, 1, v], am[:, h, TP:3 * P], start=False, stop=True,
                                   skip_group_check=True)
                mm.then_inc(done, 1)

            def kd_nat(half):
                out, done = fill("kd_nat", half)
                pe.wait_ge(kd_new, 1)
                for h in range(H_GLA):
                    mm = pe.transpose(out[:, h * P:(h + 1) * P], qe[:, h, half * P:(half + 1) * P],
                                      ident[:, :])
                mm.then_inc(done, 1)

            def state_(pair):
                out, done = fill("state", pair)
                taken(pe, "kd_nat", 0)
                taken(pe, "kd_nat", 1)
                for i in range(2):
                    h = 2 * pair + i
                    for half in range(2):
                        mm = pe.matmul(out[:, i * DV:(i + 1) * DV], kdn[:, half, h * DK:(h + 1) * DK],
                                       vgn[:, half, h * DV:(h + 1) * DV], start=half == 0, stop=half == 1,
                                       skip_group_check=True)
                mm.then_inc(done, 1)

            def rec_out(b):
                out, done = fill("rec_out", b)
                pe.wait_ge(st_new, b + 1)
                for h in range(H_GLA):
                    for t in range(2):
                        mm = pe.matmul(out[:, 2 * h + t:2 * h + t + 1],
                                       stream[:, b % 4, h * DV + t * P:h * DV + (t + 1) * P],
                                       proj["qg"][:, h, TP + b:TP + b + 1], start=True, stop=True,
                                       skip_group_check=True)
                mm.then_inc(done, 1)

            def score(h):
                out, done = fill("score", h)
                m = max(i for i, (_, b, t) in enumerate(BLOCKS) if (b, t) == ("ka", 4 * (h // 8)))
                pe.wait_ge(proj_new, TILES_BEFORE["in", m] + CN_T)
                r = slice(HD * (h % 2), HD * (h % 2) + HD)
                q, k = proj["qa"][r, h // 2, :], proj["ka"][r, h // 2, :]
                pe.matmul(out[:, 0:P], q[:, 0:P], k[:, 0:P], start=True, stop=True, skip_group_check=True)
                pe.matmul(out[:, P:3 * P], q[:, P:TP], k[:, 0:TP], start=True, stop=True,
                          skip_group_check=True).then_inc(done, 1)

            def probs_t(h):
                out, done = fill("probs_t", h)
                pe.wait_ge(p_new, h + 1)
                for i in range(3):
                    mm = pe.transpose(out[:, i * P:(i + 1) * P], sm[:, h % 2, i * P:(i + 1) * P], ident[:, :])
                mm.then_inc(done, 1)

            def values(h):
                bank, done = fill("values", h)
                taken(pe, "probs_t", h)
                for half in range(2):
                    taken(pe, "nat", ("va", half, h // 8))
                out = bank[HD * (h % 2):HD * (h % 2) + HD, :]
                v = slice(h * HD, (h + 1) * HD)
                pe.matmul(out[:, 0:TP], van[:, 0, v], pt[:, 0:TP], start=True, stop=False,
                          skip_group_check=True)
                pe.matmul(out[:, P:TP], van[:, 1, v], pt[:, TP:3 * P], start=False, stop=True,
                          skip_group_check=True).then_inc(done, 1)

            def s_scores(_):
                out, done = fill("s_scores", 0)
                pe.wait_ge(sc_new, 2 * TS)
                pe.wait_ge(self_new, 1)
                for t in range(2):
                    pe.transpose(out[:, t * P:(t + 1) * P], sc_s[:, t, :, :].rearrange("p h b -> p (h b)"),
                                 ident[:, :])
                pe.matmul(out[:, TP:TP + 1], prod[:, 0:P], ones[:, 0, :], start=True, stop=True,
                          skip_group_check=True).then_inc(done, 1)

            def s_probs(_):
                out, done = fill("s_probs", 0)
                pe.wait_ge(sp_new, 1)
                for t in range(2):
                    pe.transpose(out[:, t * P:(t + 1) * P], sm_s[:, t * P:(t + 1) * P], ident[:, :])
                pe.matmul(out[:, TP:TP + P], ones[:, 0, :].to_broadcast([P, P]), prod[:, 128:256],
                          start=True, stop=True, skip_group_check=True).then_inc(done, 1)

            held = {}

            def s_values(_):
                bank, held["done"] = fill("s_values", 0)
                held["out"] = bank[:, 0:AT_T * TS].rearrange("p (f b) -> p f b", f=AT_T)

            def s_value(b):
                pe.wait_ge(weighted, 3 * b + 3)
                for f in range(AT_T):
                    mm = pe.matmul(held["out"][:, f, b:b + 1], stream[:, (2 * b) % 4, f * P:(f + 1) * P],
                                   ones[:, 0, :], start=True, stop=True, skip_group_check=True)
                if b < TS - 1:
                    mm.then_inc(v_used, 1)
                else:
                    mm.then_inc(held["done"], 1)

            def mean_att(_):
                out, done = fill("mean_att", 0)
                pe.wait_ge(asq_new, AT_T + 1)
                pe.matmul(out[:, 0:T], ones[:, 2, :].to_broadcast([P, P]), root[:, :], start=True,
                          stop=True).then_inc(done, 1)

            def gla_mean(h):
                out, done = fill("gla_mean", h)
                pe.wait_ge(gss_new, h + 1)
                pe.matmul(out[:, 0:T], ones[:, 3, :].to_broadcast([P, P]), sqg[:, h, :], start=True,
                          stop=True).then_inc(done, 1)

            def mix_mean(_):
                _, done = fill("mean", "mix")
                mean(2, done)

            for n, (kind, m, j, last) in enumerate(CHUNKS):
                c = MIX + n
                if kind == "lr":
                    if j == 0:
                        lr_out, lr_done = fill("lowrank", 0)
                    pe.wait_ge(lo_done, c + (RING + 1))
                    for t in range(KT // 2):
                        kt = KT // 2 * j + t
                        hi = wh[:, c % RING, :, :].rearrange("p a b -> p (a b)")[:, t * P:(t + 1) * P]
                        lo = wl[:, c % RING, :, :].rearrange("p a b -> p (a b)")[:, t * P:(t + 1) * P]
                        pe.matmul(lr_out[:, 0:T], hi, xh[:, kt, :], start=kt == 0, stop=False)
                        pe.matmul(lr_out[:, 0:T], hi, xl[:, kt, :], start=False, stop=False)
                        mm = pe.matmul(lr_out[:, 0:T], lo, xh[:, kt, :], start=False, stop=kt == KT - 1)
                    mm.then_inc(used, 1)
                    if j == 1:
                        pe.wait_ge(used, c + 1 + RING)
                        pe.sem_inc(lr_done, 1)
                else:
                    before_n = TILES_BEFORE[kind, m]

                    def bank_read(t, b=before_n):
                        if b:
                            pe.wait_ge(proj_new, b - CN_T + t + 1)

                    if n == 0:
                        pe.wait_ge(x_new, 7)
                    if kind == "in":
                        if m == 0 and j % 2 == 0:
                            pe.wait_ge(xl_new, 4 + j // 2 + 1)
                        rhs = lambda t, j=j: (xh[:, CK_T * j + t, :], xl[:, CK_T * j + t, :])
                        first = j == 0
                    elif kind == "gla":
                        pe.wait_ge(og_fin, j // 2 + 1)
                        rhs = lambda t, j=j: (gh[:, CK_T * j + t, :], gl[:, CK_T * j + t, :])
                    else:
                        pe.wait_ge(atl_new, AT_T + 1)
                        rhs = lambda t, j=j: (ath[:, CK_T * j + t, :], atl[:, CK_T * j + t, :])
                    multiply(c, c % RING, rhs, lambda t: g0[:, t, 0:T], j == 0, last,
                             bank_read if j == 0 else None, last)
                for step, arg in PLAN.get(n, ()):
                    if step == "mean":
                        mix_mean(arg)
                    elif step == "nat":
                        nat(*arg)
                    elif step == "gate":
                        gate(arg)
                    elif step == "cum":
                        cumulate(arg)
                    elif step == "level_out":
                        level_out(arg)
                    elif step == "gla_out":
                        gla_out(arg)
                    elif step == "kd_nat":
                        kd_nat(arg)
                    elif step == "state":
                        state_(arg)
                    elif step == "rec_out":
                        rec_out(arg)
                    elif step == "score":
                        score(arg)
                    elif step == "probs_t":
                        probs_t(arg)
                    elif step == "values":
                        values(arg)
                    elif step == "s_scores":
                        s_scores(arg)
                    elif step == "s_probs":
                        s_probs(arg)
                    elif step == "s_values":
                        s_values(arg)
                    elif step == "s_value":
                        s_value(arg)
                    elif step == "mean_att":
                        mean_att(arg)
                    elif step == "gla_mean":
                        gla_mean(arg)

            ffn_in(1, FI2)
            def turn_out(q):
                pe.wait_ge(fin_g, q + 1)
                g = groups[q % 2]
                for half in range(3):
                    rows_n, cols = (P, slice(half * P, (half + 1) * P)) if half < 2 else (TS, slice(TP, T))
                    for n in range(4):
                        mm = pe.transpose(g[0:rows_n, half, n * P:(n + 1) * P], x[:, 4 * q + n, cols],
                                          ident[:, :])
                mm.then_inc(fin_turned, 1)

            for k in range(FO_BLOCKS * FO_CH):
                q, j = k // FO_CH, k % FO_CH
                if j == 0:
                    if q < 2:
                        pe.wait_ge((gate_in, up_in)[q], 2 * FI_BLOCKS)
                    else:
                        pe.wait_ge(fin_rows, q - 1)
                ffn_out_chunk(1, FO2 + k, q, j, (FO2 + k) % RING)
                if j == 6 and q:
                    turn_out(q - 1)
            pe.wait_ge(ssq_new, 16)
            for half in range(3):
                n, cols = (P, slice(half * P, (half + 1) * P)) if half < 2 else (TS, slice(TP, T))
                mm = pe.matmul(g0[0:n, 3, half:half + 1], ssq[:, cols], ones[:, 1, :], start=True,
                               stop=True, skip_group_check=True)
            mm.then_inc(fmean_full, 1)
            turn_out(FO_BLOCKS - 1)

        @block.scalar
        def _(act):
            def split(c, slot, loads, narrow=False):
                act.wait_ge(raw_full[slot], loads * 16)
                act.wait_ge(used, c + 1)
                src, dst = raw[:, slot, :, :], wh[:, slot, :, :]
                if narrow:
                    src = src.rearrange("p a b -> p (a b)")[:, 0:KT // 2 * RANK].rearrange(
                        "p (a b) -> p a b", b=RANK)
                    dst = dst.rearrange("p a b -> p (a b)").rearrange("p (a b) -> p a b", b=P)[:, :, 0:RANK]
                act.activation(dst, src, ACT.Copy).then_inc(hi_done, 1)

            def split_at(c):
                n = c - MIX
                split(c, c % RING, c // RING + 1, 0 <= n < len(CHUNKS) and CHUNKS[n][0] == "lr")

            def x_high(nth, q, gain, dyn=False):
                act.wait_ge(x_new, nth + 1)
                x_high_only(q, gain, dyn)
                act.activation(s_buf[:, :, :], x[:, bass.ds(4 * q, 4), :], ACT.Square).then_inc(sq_new, 1)

            def x_high_only(q, gain, dyn=False):
                if dyn:
                    act.sem_inc(misc, 1)
                for n in range(4):
                    a = act.activation(xh[:, bass.ds(4 * q + n, 1), :], x[:, bass.ds(4 * q + n, 1), :], ACT.Copy,
                                       scale=gains[:, gain, bass.ds(4 * q + n, 1)])
                a.then_inc(xh_new, 1)

            def mean_root():
                return act.activation(root[:, :], g1[:, 0, 0:T], ACT.Sqrt, bias=eps[:, 0:1])

            def ffn_in(nth, c0):
                def body(i, first):
                    for k in range(FI_BODY):
                        c = FI_BODY * i + (c0 + k + 3)
                        split(c, (c0 + k + 3) % RING, FI_BODY // RING * i + ((c0 + k + 3) // RING + 1))
                        if first and nth == 0:
                            rest_of_x(k)
                        if first and k == 7:
                            act.wait_ge(mean_full, 1 + nth)
                            mean_root().then_inc(root_new, 1)
                        if k == 8:
                            act.wait_ge(gate_in, i + (FI_BLOCKS * nth + 1))
                            act.activation(s_buf[:, :, :], s_buf[:, :, :], ACT.Silu).then_inc(gate_silu, 1)
                        if k == FI_BODY - 1:
                            act.wait_ge(u_new, i + (FI_BLOCKS * nth + 1))
                            act.sem_inc(misc, 1)
                            act.activation(uh[:, bass.ds(4 * i, 4), :], t_buf[:, :, :], ACT.Copy).then_inc(uh_new, 1)
                body(0, True)
                with act.Fori(1, FI_BLOCKS) as i:
                    body(i, False)

            act.dma_start(ident[:, :], c_ident).then_inc(ident_in, 16)
            n = 0
            for g in (g_ffn1[0], g_mix[0], g_ffn2[0], g_final, g_att[0], g_gla[0]):
                k = g.shape[0] // P
                act.dma_start(gain_rows[n:n + k, :], g.rearrange("(k p) -> k p", p=P)).then_inc(gains_in, 16)
                n += k
            act.wait_ge(gains_new, 1)
            act.wait_ge(eps_set, 1)

            def copy_x(q):
                act.wait_ge(x_turned, q + 1)
                act.activation(x[:, 4 * q:4 * q + 4, :], groups[q % 2][:, :, 0:T], ACT.Copy).then_inc(x_even, 1)

            def square(q):
                if q:
                    act.wait_ge(sq_part, q)
                act.activation(s_buf[:, :, :], x[:, 4 * q:4 * q + 4, :], ACT.Square).then_inc(sq_new, 1)

            copy_x(0)
            act.wait_ge(x_even, 1)
            x_high_only(0, 0)
            split_at(0)
            split_at(1)
            copy_x(2)
            act.wait_ge(x_odd, 1)
            x_high_only(1, 0)
            square(0)
            split_at(2)
            act.wait_ge(x_even, 2)
            x_high_only(2, 0)
            square(1)

            def rest_of_x(k):
                if k == 0:
                    act.wait_ge(x_odd, 2)
                    x_high_only(3, 0)
                elif k <= 2:
                    square(k + 1)

            ffn_in(0, FI1)
            act.wait_ge(uh_new, FI_BLOCKS)
            with act.Fori(0, FO_BLOCKS // 2) as i:
                for k in range(2 * FO_CH):
                    c = 2 * FO_CH * i + (FO1 + k + 3)
                    split(c, (FO1 + k + 3) % RING, 2 * FO_CH // RING * i + ((FO1 + k + 3) // RING + 1))
                    if k % FO_CH == FO_CH - 1:
                        b = k // FO_CH
                        x_high(2 * i + (4 + b), 2 * i + b, 1, dyn=True)

            n_k, n_s = [0], [0]

            def nat(name, half, grp):
                bank, done = filled(act, "nat", (name, half, grp))
                turn = USE["nat", (name, half, grp), 0]
                cols = slice(512 * grp, 512 * grp + 512)
                if half < 2 and name in ("vg", "va"):
                    dst = (vgn if name == "vg" else van)[:, half, cols]
                elif half < 2:
                    r = n_k[0] % 2
                    if n_k[0] >= 2:
                        act.wait_ge(rows_out[r], 16 * (n_k[0] // 2))
                    dst = rows[:, r, :]
                else:
                    r = n_s[0] % 2
                    if n_s[0] >= 2:
                        act.wait_ge(rowss_out[r], 16 * (n_s[0] // 2))
                    dst = rows_s[0:TS, r, :]
                act.activation(dst, bank[0:TS if half == 2 else P, 0:512], ACT.Copy).then_inc(done, 1)
                if name == "vg" and half < 2:
                    return
                act.wait_ge(free[turn[0]], turn[1] + 1)
                if half == 2:
                    heads = slice(8 * grp, 8 * grp + 8)
                    out = {"vg": lambda: rows_v[:, cols], "qa": lambda: rows_q[:, cols],
                           "ka": lambda: nk_s[0, :, 0, heads, :].rearrange("b h d -> b (h d)"),
                           "va": lambda: nv_s[0, :, 0, heads, :].rearrange("b h d -> b (h d)")}[name]()
                    act.dma_start(out, dst).then_inc(rowss_out[r], 16)
                    n_s[0] += 1
                else:
                    heads = slice(8 * grp, 8 * grp + 8)
                    out = (nk_p if name == "ka" else nv_p)[0, 0, half * P:(half + 1) * P, heads, :]
                    out = out.rearrange("t h d -> t (h d)")
                    if name == "ka":
                        act.dma_start(out, dst).then_inc(rows_out[r], 16)
                        n_k[0] += 1
                    else:
                        act.dma_start(out, dst).then_inc(van_out, 16)

            def gate(_):
                parts = []
                for half in range(3):
                    bank, _ = filled(act, "gate", 0, half)
                    w = D_GK if half < 2 else H_GLA * TS
                    dst = dif[:, 2 * half:2 * half + 2, :].rearrange("p a b -> p (a b)") if half < 2 else tiny[:, 0:w]
                    parts.append(dst)
                    act.activation(dst, bank[:, 0:w], ACT.Abs).then_inc(act_own, 1)
                for half, dst in enumerate(parts):
                    act.wait_ge(act_own, half + 1)
                    act.activation(dst, dst, ACT.Exp, scale=-1.0).then_inc(act_own, 1)
                for half, dst in enumerate(parts):
                    act.wait_ge(act_own, 3 + half + 1)
                    act.activation(dst, dst, ACT.Ln, bias=1.0).then_inc(gate_l, 1)
                act.wait_ge(free[USE["gate", 0, 2][0]], USE["gate", 0, 2][1] + 1)
                act.activation(a_s[:, :, :].rearrange("p h b -> p (h b)"), tiny[:, 0:H_GLA * TS], ACT.Exp,
                               scale=1.0 / TAU).then_inc(a_exp, 1)

            def cumulate(pair):
                bank, done = filled(act, "cum", pair)
                act.activation(cum[:, 2 * pair:2 * pair + 2, :].rearrange("p a b -> p (a b)"), bank,
                               ACT.Copy).then_inc(done, 1)

            def level_dif(n):
                w = LEVELS[n]
                act.wait_ge(dif_new, n + 1)
                d = dif[:, :, :].rearrange("p h (b s w) -> p (h b) s w", s=2, w=w)
                act.activation(d[:, :, 0, :], d[:, :, 0, :], ACT.Exp, scale=-1.0)
                act.activation(d[:, :, 1, :], d[:, :, 1, :], ACT.Exp).then_inc(dec_new, 1)

            def level_add(n):
                if n == 0:
                    act.wait_ge(cleared, 5)
                    for pair in range(2):
                        bank, done = filled(act, "level_out", 0, pair)
                        act.activation(am[:, 2 * pair:2 * pair + 2, P:TP],
                                       bank[:, 0:2 * P].rearrange("p (h t) -> p h t", h=2),
                                       ACT.Copy).then_inc(done, 1)

            def gla_out(h):
                bank, done = filled(act, "gla_out", h)
                for g in range(2):
                    taken(act, "nat", ("vg", 2, g))
                act.activation(og[:, 2 * h:2 * h + 2, 0:TP], bank.rearrange("p (a t) -> p a t", a=2),
                               ACT.Copy).then_inc(done, 1)

            def kdecay_dif(_):
                act.wait_ge(dif_new, len(LEVELS) + 1)
                act.activation(dif[:, :, :], dif[:, :, :], ACT.Exp, scale=-1.0).then_inc(dec_new, 1)

            def kd_nat(half):
                bank, done = filled(act, "kd_nat", half)
                act.activation(kdn[:, half, :], bank, ACT.Copy).then_inc(done, 1)

            def state_(pair):
                bank, done = filled(act, "state", pair)
                act.wait_ge(kd_new, 1)
                act.activation(sfin[:, 2 * pair:2 * pair + 2, :].rearrange("p a b -> p (a b)"), bank,
                               ACT.Copy).then_inc(done, 1)

            def rec_out(b):
                bank, done = filled(act, "rec_out", b)
                act.activation(og[:, :, TP + b], bank[:, 0:2 * H_GLA], ACT.Copy).then_inc(done, 1)
                act.wait_ge(st_new, b + 1)
                act.dma_start(ns_s[0, b].rearrange("h k v -> k h v"),
                              stream[:, b % 4, :].rearrange("p (h v) -> p h v", h=H_GLA)).then_inc(st_out[b % 4], 16)

            def exp(h):
                act.wait_ge(masked, h + 1)
                one, two, t0 = sm[:, h % 2, 0:P], sm[:, h % 2, P:3 * P], 8 * (h % 2)
                act.activation(one, one, ACT.Exp, scale=HD ** -0.5, bias=tiny[:, t0 + 2:t0 + 3])
                act.activation(two, two, ACT.Exp, scale=HD ** -0.5, bias=tiny[:, t0 + 3:t0 + 4]).then_inc(e_new, 1)

            def probs_t(h):
                bank, done = filled(act, "probs_t", h)
                if h:
                    bank_v, k = USE["values", h - 1, 0]
                    act.wait_ge(full[bank_v], k + 1)
                act.activation(pt[:, :], bank[:, 0:3 * P], ACT.Copy).then_inc(done, 1)

            def values(h):
                bank, done = filled(act, "values", h)
                r = slice(HD * (h % 2), HD * (h % 2) + HD)
                act.activation(proj["qa"][r, h // 2, 0:TP], bank[r, 0:TP], ACT.Copy).then_inc(done, 1)

            def att_split(f):
                taken(act, "values", 2 * f + 1)
                if f:
                    act.wait_ge(asq_new, f)
                act.activation(ath[:, f, 0:TP], proj["qa"][:, f, 0:TP], ACT.Copy, scale=gatt[:, f:f + 1])
                act.activation(asq[:, 0:TP], proj["qa"][:, f, 0:TP], ACT.Square).then_inc(ath_new, 1)

            def s_scores(_):
                bank, done = filled(act, "s_scores", 0)
                act.wait_ge(smax_new, 1)
                act.activation(sm_s[:, :], bank[:, 0:TP + 1], ACT.Exp, scale=HD ** -0.5,
                               bias=tiny[:, 17:18]).then_inc(done, 1)

            def s_probs(_):
                bank, done = filled(act, "s_probs", 0)
                act.activation(pt_s[:, :, :, :].rearrange("p t h b -> p (t h b)"), bank[:, 0:TP], ACT.Copy)
                act.activation(prod[:, 256:384], bank[:, TP:TP + P], ACT.Copy).then_inc(done, 1)

            def att_split_s(_):
                act.wait_ge(oatts_new, 1)
                act.wait_ge(asq_new, AT_T)
                for f in range(AT_T):
                    act.activation(ath[:, f, TP:T], proj["qa"][:, f, TP:T], ACT.Copy, scale=gatt[:, f:f + 1])
                act.activation(tiny[:, 0:64].rearrange("p (f b) -> p f b", b=TS), proj["qa"][:, :, TP:T],
                               ACT.Square).then_inc(ath_new, 1)

            def mean_att(_):
                bank, done = filled(act, "mean_att", 0)
                act.activation(asq[:, :], bank[:, 0:T], ACT.Sqrt, bias=eps[:, 0:1]).then_inc(done, 1)

            def gla_sq(h):
                if h == 0:
                    taken(act, "rec_out", TS - 1)
                if h >= 2:
                    act.wait_ge(gss_new, h - 1)
                act.activation(rstdg[:, 2 * (h % 2):2 * (h % 2) + 2, :], og[:, 2 * h:2 * h + 2, :],
                               ACT.Square).then_inc(gsq_new, 1)

            def gla_mean(h):
                bank, done = filled(act, "gla_mean", h)
                act.wait_ge(gss_new, H_GLA)
                act.activation(rstdg[:, h, :], bank[:, 0:T], ACT.Sqrt, bias=eps[:, 0:1]).then_inc(done, 1)

            def gla_gate(g):
                act.wait_ge(proj_new, TILES_BEFORE["in", len(BLOCKS) - 2 + g] + CN_T)
                act.activation(rg[:, 4 * g:4 * g + 4, :], rg[:, 4 * g:4 * g + 4, :], ACT.Silu).then_inc(rg_silu, 1)

            def gla_split(g):
                act.wait_ge(og_new, g + 1)
                for t in range(4):
                    a = act.activation(gh[:, 4 * g + t, :], og[:, 4 * g + t, :], ACT.Copy,
                                       scale=ggla[:, t % 2:t % 2 + 1])
                a.then_inc(gh_new, 1)

            for n, (kind, m, j, last) in enumerate(CHUNKS):
                split_at(MIX + n + 3)
                if kind == "att" and last:
                    if m == 0:
                        for r in range(2):
                            act.wait_ge(rowss_out[r], 64)
                            act.wait_ge(rows_out[r], 32)
                    x_high(8 + m, m, 2)
                for step, arg in PLAN.get(n, ()):
                    if step == "mean":
                        _, done = filled(act, "mean", arg)
                        mean_root().then_inc(done, 1)
                    elif step == "nat":
                        nat(*arg)
                    elif step == "gate":
                        gate(arg)
                    elif step == "cum":
                        cumulate(arg)
                    elif step == "level_dif":
                        level_dif(arg)
                    elif step == "level_add":
                        level_add(arg)
                    elif step == "gla_out":
                        gla_out(arg)
                    elif step == "kdecay_dif":
                        kdecay_dif(arg)
                    elif step == "kd_nat":
                        kd_nat(arg)
                    elif step == "state":
                        state_(arg)
                    elif step == "rec_out":
                        rec_out(arg)
                    elif step == "exp":
                        exp(arg)
                    elif step == "probs_t":
                        probs_t(arg)
                    elif step == "values":
                        values(arg)
                    elif step == "att_split":
                        att_split(arg)
                    elif step == "s_scores":
                        s_scores(arg)
                    elif step == "s_probs":
                        s_probs(arg)
                    elif step == "att_split_s":
                        att_split_s(arg)
                    elif step == "mean_att":
                        mean_att(arg)
                    elif step == "gla_sq":
                        gla_sq(arg)
                    elif step == "gla_mean":
                        gla_mean(arg)
                    elif step == "gla_gate":
                        gla_gate(arg)
                    elif step == "gla_split":
                        gla_split(arg)

            act.wait_ge(rows_out[0], 32)
            act.wait_ge(rows_out[1], 32)
            act.wait_ge(rowss_out[0], 64)
            act.wait_ge(rowss_out[1], 64)
            act.wait_ge(van_out, 64)
            act.wait_ge(stored, 1)
            ffn_in(1, FI2)
            def rows_out_(q):
                act.wait_ge(fin_turned, q + 1)
                g = groups[q % 2]
                for half in range(2):
                    act.activation(yn[:, half, 512 * q:512 * q + 512], g[:, half, :], ACT.Copy)
                act.activation(yns[0:TS, 512 * q:512 * q + 512], g[0:TS, 2, :], ACT.Copy).then_inc(fin_rows, 1)

            for k in range(FO_BLOCKS * FO_CH):
                q, j = k // FO_CH, k % FO_CH
                if FO2 + k + 3 < END:
                    split_at(FO2 + k + 3)
                if j == 10 and q:
                    rows_out_(q - 1)
                if j == FO_CH - 1:
                    act.wait_ge(x_new, 13 + q)
                    act.wait_ge(sq_part, 12 + q)
                    act.activation(s_buf[:, :, :], x[:, 4 * q:4 * q + 4, :], ACT.Square).then_inc(sq_new, 1)
            act.activation(root[:, 0:1], eps[:, 0:1], ACT.Sqrt)
            act.wait_ge(fmean_full, 1)
            for half in range(3):
                n = P if half < 2 else TS
                a = act.activation(tiny[0:n, half:half + 1], g0[0:n, 3, half:half + 1], ACT.Sqrt, bias=eps[0:n, 0:1])
            a.then_inc(froot, 1)
            act.wait_ge(frstd, 3)
            q, g = FO_BLOCKS - 1, groups[(FO_BLOCKS - 1) % 2]
            act.wait_ge(fin_turned, q + 1)
            for half in range(2):
                act.activation(yn[:, half, 512 * q:512 * q + 512], g[:, half, :], ACT.Copy,
                               scale=tiny[:, 4 + half:5 + half]).then_inc(fin_rows, 1)
            act.activation(yns[0:TS, 512 * q:512 * q + 512], g[0:TS, 2, :], ACT.Copy,
                           scale=tiny[0:TS, 6:7]).then_inc(fin_rows, 1)

        @block.vector
        def _(dve):
            def low(c, slot, narrow=False):
                dve.wait_ge(hi_done, c + 1)
                src, h, dst = raw[:, slot, :, :], wh[:, slot, :, :], wl[:, slot, :, :]
                if narrow:
                    src = src.rearrange("p a b -> p (a b)")[:, 0:KT // 2 * RANK].rearrange(
                        "p (a b) -> p a b", b=RANK)
                    h, dst = (v.rearrange("p a b -> p (a b)").rearrange("p (a b) -> p a b", b=P)[:, :, 0:RANK]
                              for v in (h, dst))
                dve.tensor_tensor(dst, src, h.bitcast(F32), ALU.subtract).then_inc(lo_done, 1)

            def low_at(c):
                n = c - MIX
                low(c, c % RING, 0 <= n < len(CHUNKS) and CHUNKS[n][0] == "lr")

            links = [0]

            def link(ins):
                links[0] += 1
                ins.then_inc(vec, 1)
                dve.wait_ge(vec, links[0])

            def update(q, grp, c_end):
                dve.wait_ge(used, c_end + (1 + RING))
                xq = x[:, bass.ds(4 * q, 4), :]
                dve.scalar_tensor_tensor(out=xq, in0=groups[grp][:, :, 0:T], scalar=0.5, in1=xq,
                                         op0=ALU.mult, op1=ALU.add).then_inc(x_new, 1)

            def add_squares(nth):
                dve.wait_ge(sq_new, nth + 1)
                if type(nth) is not int or nth:
                    dve.wait_ge(ssq_new, nth)
                dve.tensor_reduce(t_buf[:, 0, :], s_buf[:, :, :].rearrange("p k t -> p t k"), AX_X,
                                  ALU.add).then_inc(sq_part, 1)
                dve.wait_ge(sq_part, nth + 1)
                dve.tensor_tensor(ssq[:, :], ssq[:, :], t_buf[:, 0, :], ALU.add).then_inc(ssq_new, 1)

            def x_low(nth, q, gain, sums=True):
                dve.wait_ge(xh_new, nth + 1)
                for n in range(4):
                    t = bass.ds(4 * q + n, 1)
                    a = dve.scalar_tensor_tensor(out=xl[:, t, :], in0=x[:, t, :], scalar=gains[:, gain, t],
                                                 in1=xh[:, t, :].bitcast(F32), op0=ALU.mult, op1=ALU.subtract)
                a.then_inc(xl_new, 1)
                if sums:
                    add_squares(nth)

            def clear_squares():
                link(dve.memset(ssq[:, :], 0.0))

            def factor(nth):
                dve.reciprocal(rstd[:, :], root[:, :]).then_inc(rstd_new, 1)
                dve.wait_ge(rstd_new, nth)

            def wide(v, n=4):
                return v.unsqueeze(1).to_broadcast([P, n, T])

            def ffn_in(nth, c0):
                def body(i, first):
                    for k in range(FI_BODY):
                        low(FI_BODY * i + (c0 + k + 3), (c0 + k + 3) % RING)
                        if first and nth == 0:
                            rest_of_x(k)
                        if k == 7:
                            if first:
                                dve.wait_ge(root_new, 1 + nth)
                                factor(1 + 2 * nth)
                                clear_squares()
                            dve.wait_ge(used, FI_BODY * i + (c0 + FI_BODY // 2 + RING))
                            dve.tensor_tensor(s_buf[:, :, :], g0[:, :, 0:T], wide(rstd[:, :]),
                                              ALU.mult).then_inc(gate_in, 1)
                        if k == FI_BODY - 1:
                            dve.wait_ge(used, FI_BODY * i + (c0 + FI_BODY + RING))
                            if not first:
                                dve.wait_ge(uh_new, i + FI_BLOCKS * nth)
                            dve.tensor_tensor(t_buf[:, :, :], g1[:, :, 0:T], wide(rstd[:, :]),
                                              ALU.mult).then_inc(up_in, 1)
                            dve.wait_ge(up_in, i + (FI_BLOCKS * nth + 1))
                            dve.wait_ge(gate_silu, i + (FI_BLOCKS * nth + 1))
                            dve.tensor_tensor(t_buf[:, :, :], t_buf[:, :, :], s_buf[:, :, :],
                                              ALU.mult).then_inc(u_new, 1)
                            dve.wait_ge(u_new, i + (FI_BLOCKS * nth + 1))
                            dve.wait_ge(uh_new, i + (FI_BLOCKS * nth + 1))
                            dve.tensor_tensor(ul[:, bass.ds(4 * i, 4), :], t_buf[:, :, :],
                                              uh[:, bass.ds(4 * i, 4), :].bitcast(F32),
                                              ALU.subtract).then_inc(ul_new, 1)
                body(0, True)
                with dve.Fori(1, FI_BLOCKS) as i:
                    body(i, False)

            dve.memset(eps[:, :], EPS).then_inc(eps_set, 1)
            dve.sem_inc(lo_done, RING)
            dve.wait_ge(gains_full, 1)
            dve.tensor_copy(all_gains[:, :], g1[:, 3, 0:4 * KT + AT_T + DV // P]).then_inc(gains_new, 1)
            dve.wait_ge(gains_new, 1)
            clear_squares()

            def copy_x(q):
                dve.wait_ge(x_turned, q + 1)
                dve.tensor_copy(x[:, 4 * q:4 * q + 4, :], groups[q % 2][:, :, 0:T]).then_inc(x_odd, 1)

            copy_x(1)
            x_low(0, 0, 0, sums=False)
            low_at(0)
            low_at(1)
            copy_x(3)
            x_low(1, 1, 0, sums=False)
            add_squares(0)
            low_at(2)
            x_low(2, 2, 0, sums=False)

            def rest_of_x(k):
                if k == 0:
                    add_squares(1)
                    dve.wait_ge(x_odd, 2)
                    x_low(3, 3, 0, sums=False)
                elif k <= 2:
                    add_squares(k + 1)
                    if k == 2:
                        dve.sem_inc(x_new, 4)

            ffn_in(0, FI1)
            with dve.Fori(0, FO_BLOCKS // 2) as i:
                for k in range(2 * FO_CH):
                    low(2 * FO_CH * i + (FO1 + k + 3), (FO1 + k + 3) % RING)
                    if k % FO_CH == FO_CH - 1:
                        b = k // FO_CH
                        update(2 * i + b, b, 2 * FO_CH * i + (FO1 + k))
                        x_low(2 * i + (4 + b), 2 * i + b, 1)

            def take_tiles(n, kind, m, last_c):
                b0 = TILES_BEFORE[kind, m]
                sent = b0 // CN_T * (CN_T - 1)
                for t in range(CN_T):
                    if t < CN_T - 1:
                        dve.wait_ge(tiles, sent + t + 1)
                    else:
                        dve.wait_ge(used, last_c + 1 + RING)
                    src = g0[:, t, 0:T]
                    if kind == "in":
                        _, name, t0 = BLOCKS[m]
                        dst = proj[name][:, t0 + t, :]
                        if name == "qg":
                            a = dve.scalar_tensor_tensor(out=dst, in0=src, scalar=DK ** -0.5, in1=rstd[:, :],
                                                         op0=ALU.mult, op1=ALU.mult)
                        else:
                            a = dve.tensor_tensor(dst, src, rstd[:, :], ALU.mult)
                        a.then_inc(proj_new, 1)
                    elif kind == "gla":
                        xt = x[:, 4 * m + t, :]
                        dve.tensor_tensor(xt, src, xt, ALU.add).then_inc(proj_new, 1)
                    else:
                        dve.tensor_tensor(t_buf[:, t, :], src, asq[:, :], ALU.mult).then_inc(proj_new, 1)
                if kind == "att":
                    dve.wait_ge(proj_new, b0 + CN_T)
                    xq = x[:, 4 * m:4 * m + 4, :]
                    dve.tensor_tensor(xq, t_buf[:, :, :], xq, ALU.add).then_inc(x_new, 1)

            def lowrank(_):
                bank, done = filled(dve, "lowrank", 0)
                dve.wait_ge(cleared, 5)
                dve.tensor_tensor(lowr[0:RANK, :], bank[0:RANK, 0:T], rstd[0:RANK, :], ALU.mult).then_inc(done, 1)

            def gate(_):
                for half in range(3):
                    bank, done = filled(dve, "gate", 0, half)
                    dve.wait_ge(gate_l, half + 1)
                    w = D_GK if half < 2 else H_GLA * TS
                    l = dif[:, 2 * half:2 * half + 2, :].rearrange("p a b -> p (a b)") if half < 2 else tiny[:, 0:w]
                    dst = la[:, half, :] if half < 2 else tiny[:, 0:w]
                    dve.scalar_tensor_tensor(out=dst, in0=bank[:, 0:w], scalar=0.0, in1=l, op0=ALU.min,
                                             op1=ALU.subtract).then_inc(done, 1)

            def level_dif(n):
                w = LEVELS[n]
                if n == 0:
                    taken(dve, "cum", 0)
                    taken(dve, "cum", 1)
                    dve.wait_ge(cleared, 5)
                else:
                    dve.wait_ge(qk_new, n)
                c = cum[:, :, :].rearrange("p h (b w) -> p (h b) w", w=2 * w)
                d = dif[:, :, :].rearrange("p h (b w) -> p (h b) w", w=2 * w)
                nb = H_GLA * TP // (2 * w)
                dve.tensor_tensor(d, c, c[:, :, w - 1:w].to_broadcast([P, nb, 2 * w]),
                                  ALU.subtract).then_inc(dif_new, 1)

            def level_mul(n):
                w = LEVELS[n]
                if n:
                    bank, k = USE["level_out", n - 1, 1]
                    dve.wait_ge(full[bank], k + 1)
                dve.wait_ge(dec_new, n + 1)
                for dst, src, s in ((ke, "kg", 0), (qe, "qg", 1)):
                    o, i, d = (v.rearrange("p h (b s w) -> p h b s w", s=2, w=w)[:, :, :, s, :]
                               for v in (dst[:, :, :], proj[src][:, :, 0:TP], dif[:, :, :]))
                    a = dve.tensor_tensor(o, i, d, ALU.mult)
                a.then_inc(qk_new, 1)

            def level_add(n):
                if n == 0:
                    return
                for half in range(2):
                    taken(dve, "level_out", n - 1, half)
                    bank, done = filled(dve, "level_out", n, half)
                    dve.copy_predicated(am[:, :, 2 * P * half:2 * P * half + P],
                                        level[:, n - 1, :].unsqueeze(1).to_broadcast([P, H_GLA, P]),
                                        bank.rearrange("p (h t) -> p h t", h=H_GLA)).then_inc(done, 1)

            def kdecay_dif(_):
                dve.wait_ge(qk_new, len(LEVELS))
                dve.tensor_tensor(dif[:, :, :], cum[:, :, :],
                                  cum[:, :, TP - 1:TP].to_broadcast([P, H_GLA, TP]),
                                  ALU.subtract).then_inc(dif_new, 1)

            def kdecay_mul(_):
                bank, k = USE["level_out", len(LEVELS) - 1, 1]
                dve.wait_ge(full[bank], k + 1)
                dve.wait_ge(dec_new, len(LEVELS) + 1)
                dve.tensor_tensor(qe[:, :, :], proj["kg"][:, :, 0:TP], dif[:, :, :], ALU.mult).then_inc(kd_new, 1)

            def rec(b):
                dve.wait_ge(decayed, b + 1)
                dve.wait_ge(bc_in[b % 2], 16 * (b // 2 + 1))
                for h in range(H_GLA):
                    st = stream[:, b % 4, h * DV:(h + 1) * DV]
                    a = dve.scalar_tensor_tensor(out=st, in0=bcast[:, b % 2, h * DV:(h + 1) * DV],
                                                 scalar=proj["kg"][:, h, TP + b:TP + b + 1], in1=st,
                                                 op0=ALU.mult, op1=ALU.add)
                a.then_inc(st_new, 1)

            def score(h):
                bank, done = filled(dve, "score", h)
                if h == 0:
                    dve.wait_ge(attc_in, 32)
                    taken(dve, "gate", 0, 2)
                elif h >= 2:
                    b, k = USE["probs_t", h - 2, 0]
                    dve.wait_ge(full[b], k + 1)
                one, two, t0 = slice(0, P), slice(P, 3 * P), 8 * (h % 2)
                dve.tensor_tensor_reduce(sm[:, h % 2, one], bank[:, one], mask[:, one], 1.0, NEG, ALU.add,
                                         ALU.max, tiny[:, t0:t0 + 1])
                dve.tensor_tensor_reduce(sm[:, h % 2, two], bank[:, two], mask[:, two], 1.0, NEG, ALU.add,
                                         ALU.max, tiny[:, t0 + 1:t0 + 2]).then_inc(done, 1)
                taken(dve, "score", h)
                dve.tensor_scalar(tiny[:, t0 + 2:t0 + 4], tiny[:, t0:t0 + 2], -HD ** -0.5, None,
                                  ALU.mult).then_inc(masked, 1)

            def norm(h):
                one, two, t0 = sm[:, h % 2, 0:P], sm[:, h % 2, P:3 * P], 8 * (h % 2)
                dve.wait_ge(e_new, h + 1)
                dve.tensor_tensor_reduce(one, one, mult[:, 0:P], 1.0, 0.0, ALU.mult, ALU.add,
                                         tiny[:, t0 + 4:t0 + 5])
                link(dve.tensor_tensor_reduce(two, two, mult[:, P:3 * P], 1.0, 0.0, ALU.mult, ALU.add,
                                              tiny[:, t0 + 5:t0 + 6]))
                link(dve.reciprocal(tiny[:, t0 + 6:t0 + 8], tiny[:, t0 + 4:t0 + 6]))
                dve.tensor_scalar(one, one, tiny[:, t0 + 6:t0 + 7], None, ALU.mult)
                dve.tensor_scalar(two, two, tiny[:, t0 + 7:t0 + 8], None, ALU.mult).then_inc(p_new, 1)

            def att_split(f):
                dve.wait_ge(ath_new, f + 1)
                if f == 0:
                    link(dve.memset(root[:, :], 0.0))
                dve.scalar_tensor_tensor(out=atl[:, f, 0:TP], in0=proj["qa"][:, f, 0:TP], scalar=gatt[:, f:f + 1],
                                         in1=ath[:, f, 0:TP].bitcast(F32), op0=ALU.mult,
                                         op1=ALU.subtract).then_inc(atl_new, 1)
                if f:
                    dve.wait_ge(asq_new, f)
                dve.tensor_tensor(root[:, 0:TP], root[:, 0:TP], asq[:, 0:TP], ALU.add).then_inc(asq_new, 1)

            def cache_k(b):
                for t in range(2):
                    n = 2 * b + t
                    dve.wait_ge(prod_new, n + 1)
                    dve.tensor_reduce(sc_s[:, t, :, b], stream[:, n % 4, :].rearrange("p (h d) -> p h d", d=HD),
                                      AX_X, ALU.add).then_inc(sc_new, 1)

            def self_score(_):
                for name in ("qa", "ka"):
                    m = max(i for i, (_, b, t) in enumerate(BLOCKS) if (b, t) == (name, 4))
                    dve.wait_ge(proj_new, TILES_BEFORE["in", m] + CN_T)
                link(dve.memset(prod[:, 0:P], 0.0))
                for e in range(2):
                    r = slice(HD * e, HD * e + HD)
                    dst = prod[r, 0:P].rearrange("p (f e b) -> p f e b", e=2, b=TS)[:, :, e, :]
                    a = dve.tensor_tensor(dst, proj["qa"][r, :, TP:T], proj["ka"][r, :, TP:T], ALU.mult)
                a.then_inc(self_new, 1)

            def s_scores(_):
                bank, _ = filled(dve, "s_scores", 0)
                link(dve.tensor_reduce(tiny[:, 16:17], bank[:, 0:TP + 1], AX_X, ALU.max))
                dve.tensor_scalar(tiny[:, 17:18], tiny[:, 16:17], -HD ** -0.5, None, ALU.mult).then_inc(smax_new, 1)

            def s_norm(_):
                taken(dve, "s_scores", 0)
                dve.wait_ge(sconst_in, 16)
                link(dve.tensor_tensor_reduce(sm_s[:, :], sm_s[:, :], smult[:, :], 1.0, 0.0, ALU.mult, ALU.add,
                                              tiny[:, 18:19]))
                link(dve.reciprocal(tiny[:, 19:20], tiny[:, 18:19]))
                link(dve.tensor_scalar(sm_s[:, :], sm_s[:, :], tiny[:, 19:20], None, ALU.mult))
                dve.tensor_scalar(prod[:, 128:256], ident[:, :], sm_s[:, TP:TP + 1], None,
                                  ALU.mult).then_inc(sp_new, 1)

            def own_value(_):
                bank, done = filled(dve, "s_values", 0)
                taken(dve, "s_probs", 0)
                for e in range(2):
                    r = slice(HD * e, HD * e + HD)
                    own = prod[r, 256:384].rearrange("p (f e b) -> p f e b", e=2, b=TS)[:, :, e, :]
                    tmp = prod[r, 384:448].rearrange("p (f b) -> p f b", b=TS)
                    link(dve.tensor_tensor(tmp, own, proj["va"][r, :, TP:T], ALU.mult))
                    src = bank[r, 0:AT_T * TS].rearrange("p (f b) -> p f b", b=TS)
                    a = dve.tensor_tensor(proj["qa"][r, :, TP:T], src, tmp, ALU.add)
                    if e == 0:
                        link(a)
                    else:
                        a.then_inc(done, 1)
                taken(dve, "s_values", 0)
                dve.sem_inc(oatts_new, 1)

            def att_split_s(_):
                dve.wait_ge(ath_new, AT_T + 1)
                for f in range(AT_T):
                    a = dve.scalar_tensor_tensor(out=atl[:, f, TP:T], in0=proj["qa"][:, f, TP:T],
                                                 scalar=gatt[:, f:f + 1], in1=ath[:, f, TP:T].bitcast(F32),
                                                 op0=ALU.mult, op1=ALU.subtract)
                a.then_inc(atl_new, 1)
                dve.tensor_reduce(root[:, TP:T], tiny[:, 0:64].rearrange("p (f b) -> p b f", b=TS), AX_X,
                                  ALU.add).then_inc(asq_new, 1)

            def mean_att(_):
                taken(dve, "mean_att", 0)
                dve.reciprocal(asq[:, :], asq[:, :]).then_inc(arstd_new, 1)

            def gla_sq(h):
                dve.wait_ge(gsq_new, h + 1)
                dve.tensor_tensor(sqg[:, h, :], rstdg[:, 2 * (h % 2), :], rstdg[:, 2 * (h % 2) + 1, :],
                                  ALU.add).then_inc(gss_new, 1)

            def gla_mean(h):
                taken(dve, "gla_mean", h)
                link(dve.reciprocal(rstdg[:, h, :], rstdg[:, h, :]))
                o = og[:, 2 * h:2 * h + 2, :]
                dve.tensor_tensor(o, o, wide(rstdg[:, h, :], 2), ALU.mult).then_inc(grstd_new, 1)

            def gla_gate(g):
                dve.wait_ge(rg_silu, g + 1)
                dve.wait_ge(grstd_new, H_GLA)
                o = og[:, 4 * g:4 * g + 4, :]
                dve.tensor_tensor(o, o, rg[:, 4 * g:4 * g + 4, :], ALU.mult).then_inc(og_new, 1)

            def gla_split(g):
                dve.wait_ge(og_new, g + 1)
                dve.wait_ge(gh_new, g + 1)
                for t in range(4):
                    k = 4 * g + t
                    a = dve.scalar_tensor_tensor(out=gl[:, k, :], in0=og[:, 4 * g + t, :],
                                                 scalar=ggla[:, t % 2:t % 2 + 1],
                                                 in1=gh[:, k, :].bitcast(F32), op0=ALU.mult, op1=ALU.subtract)
                a.then_inc(og_fin, 1)

            for n, (kind, m, j, last) in enumerate(CHUNKS):
                low_at(MIX + n + 3)
                if last and kind != "lr":
                    if kind == "att" and m == 0:
                        dve.wait_ge(arstd_new, 1)
                        for r in range(2):
                            dve.wait_ge(rowss_out[r], 64)
                            dve.wait_ge(rows_out[r], 32)
                    take_tiles(n, kind, m, MIX + n)
                    if kind == "att":
                        x_low(8 + m, m, 2)
                for step, arg in PLAN.get(n, ()):
                    if step == "mean":
                        taken(dve, "mean", "mix")
                        factor(2)
                        clear_squares()
                    elif step == "lowrank":
                        lowrank(arg)
                    elif step == "gate":
                        gate(arg)
                    elif step == "level_dif":
                        level_dif(arg)
                    elif step == "level_mul":
                        level_mul(arg)
                    elif step == "level_add":
                        level_add(arg)
                    elif step == "kdecay_dif":
                        kdecay_dif(arg)
                    elif step == "kdecay_mul":
                        kdecay_mul(arg)
                    elif step == "rec":
                        rec(arg)
                    elif step == "score":
                        score(arg)
                    elif step == "norm":
                        norm(arg)
                    elif step == "s_norm":
                        s_norm(arg)
                    elif step == "att_split":
                        att_split(arg)
                    elif step == "cache_k":
                        cache_k(arg)
                    elif step == "self_score":
                        self_score(arg)
                    elif step == "s_scores":
                        s_scores(arg)
                    elif step == "own_value":
                        own_value(arg)
                    elif step == "att_split_s":
                        att_split_s(arg)
                    elif step == "mean_att":
                        mean_att(arg)
                    elif step == "gla_sq":
                        gla_sq(arg)
                    elif step == "gla_mean":
                        gla_mean(arg)
                    elif step == "gla_gate":
                        gla_gate(arg)
                    elif step == "gla_split":
                        gla_split(arg)

            ffn_in(1, FI2)
            for k in range(FO_BLOCKS * FO_CH):
                q, j = k // FO_CH, k % FO_CH
                if FO2 + k + 3 < END:
                    low_at(FO2 + k + 3)
                if j == FO_CH - 1:
                    update(q, q % 2, FO2 + k)
                    add_squares(12 + q)
                    for n in range(4):
                        t = 4 * q + n
                        a = dve.tensor_scalar(x[:, t, :], x[:, t, :], gains[:, 3, t:t + 1], None, ALU.mult)
                    a.then_inc(fin_g, 1)
            dve.wait_ge(froot, 1)
            for half in range(3):
                n = P if half < 2 else TS
                dve.reciprocal(tiny[0:n, 4 + half:5 + half], tiny[0:n, half:half + 1]).then_inc(frstd, 1)
            dve.wait_ge(frstd, 3)
            dve.wait_ge(fin_rows, FO_BLOCKS - 1)
            done = 512 * (FO_BLOCKS - 1)
            for half in range(2):
                dve.tensor_scalar(yn[:, half, 0:done], yn[:, half, 0:done], tiny[:, 4 + half:5 + half], None,
                                  ALU.mult).then_inc(y_new, 1)
            dve.tensor_scalar(yns[0:TS, 0:done], yns[0:TS, 0:done], tiny[0:TS, 6:7], None, ALU.mult).then_inc(y_new, 1)

        @block.gpsimd
        def _(pool):
            pool.sem_inc(used, RING)
            pool.dma_start(ones[:, :, :], c_ones.rearrange("p (a b) -> p a b", b=1)).then_inc(consts_in, 16)
            pool.dma_start(smult[:, :], c_smult).then_inc(sconst_in, 16)
            pool.wait_ge(used, MIX + RING)
            pool.dma_start(wg2[0:RANK, :], w_gate2[0]).then_inc(wg2_in, 16)
            pool.dma_start(wg2[RANK:RANK + 1, :], b_gate2).then_inc(wg2_in, 16)
            pool.dma_start(cumw[:, :], c_cum).then_inc(glac_in, 16)
            pool.dma_start(level_f[:, :, :], c_level).then_inc(glac_in, 16)
            pool.memset(lowr[0:32, :], 1.0).then_inc(cleared, 1)
            pool.memset(qe[:, :, :], 0.0).then_inc(cleared, 1)
            pool.memset(ke[:, :, :], 0.0).then_inc(cleared, 1)
            pool.wait_ge(glac_in, 32)
            pool.tensor_copy(level[:, :, :], level_f[:, :, :]).then_inc(cleared, 1)
            pool.wait_ge(cleared, 4)
            pool.memset(am[:, :, :], 0.0).then_inc(cleared, 1)
            for h in range(H_GLA):
                if h % 2 == 0:
                    taken(pool, "state", h // 2)
                pool.dma_start(ns_p[0, 0, h], sfin[:, h, :]).then_inc(sfin_out, 16)
            taken(pool, "gla_out", H_GLA - 1)
            pool.wait_ge(sfin_out, 64)
            pool.dma_start(mult[:, :], c_mult).then_inc(attc_in, 16)
            pool.dma_start(mask[:, :], c_mask).then_inc(attc_in, 16)
            pool.wait_ge(a_exp, 1)
            for b in range(TS):
                pool.wait_ge(st_in[b % 4], 16 * (b // 4 + 1))
                for h in range(H_GLA):
                    st = stream[:, b % 4, h * DV:(h + 1) * DV]
                    a = pool.tensor_scalar(st, st, a_s[:, h, b:b + 1], None, ALU.mult)
                a.then_inc(decayed, 1)
            for b in range(TS):
                pool.wait_ge(bc_in[b % 2], 16 * (TS // 2 + b // 2 + 1))
                for t in range(2):
                    slot = (2 * b + t) % 4
                    pool.wait_ge(kc_in[slot], cache_count(b, t, False))
                    pool.tensor_tensor(stream[:, slot, :], stream[:, slot, :], bcast[:, b % 2, :],
                                       ALU.mult).then_inc(prod_new, 1)
            taken(pool, "s_probs", 0)
            for b in range(TS):
                for t in range(2):
                    slot = (2 * b + t) % 4
                    pool.wait_ge(kc_in[slot], cache_count(b, t, True))
                    v = stream[:, slot, :].rearrange("p (h d) -> p h d", d=HD)
                    pool.tensor_tensor(v, v, pt_s[:, t, :, b:b + 1].to_broadcast([P, H_ATT, HD]),
                                       ALU.mult).then_inc(weighted, 1)
                pool.wait_ge(weighted, 3 * b + 2)
                one, two = stream[:, (2 * b) % 4, :], stream[:, (2 * b + 1) % 4, :]
                pool.tensor_tensor(one, one, two, ALU.add).then_inc(weighted, 1)
            pool.sem_inc(stored, 1)


_INS = ["x_prompt", "x_sample", "cache_att_k", "cache_att_v", "state_gla", "g_ffn1", "w_ffn1_in",
        "w_ffn1_out", "g_mix", "w_in", "w_gate2", "b_gate2", "g_att_out", "g_gla_out", "w_out", "g_ffn2",
        "w_ffn2_in", "w_ffn2_out", "g_final"]
_OUTS = [(1, TP, D), (TS, 1, D), (1, 1, TP, H_ATT, HD), (1, 1, TP, H_ATT, HD), (1, 1, H_GLA, DK, DV),
         (1, TS, 1, H_ATT, HD), (1, TS, 1, H_ATT, HD), (1, TS, H_GLA, DK, DV)]


def shape_constants():
    import numpy as np
    ident = np.eye(P, dtype=np.float32)
    ones = np.tile(np.array([1, 1 / D, 1 / D_ATT, 1 / DV], np.float32), (P, 1))
    s, t = np.arange(P)[:, None], np.arange(TP)[None, :]
    cum = np.where(s <= t, np.float32(1 / TAU), np.float32(0))
    level = np.zeros((P, len(LEVELS), P), np.float32)
    s, t = np.arange(P)[:, None], np.arange(P)[None, :]
    for n, w in enumerate(LEVELS[1:]):
        level[:, n] = (s // (2 * w) == t // (2 * w)) & (s % (2 * w) < w) & (t % (2 * w) >= w)
    level[:, -1] = s == t
    mult = np.zeros((P, 3 * P), np.float32)
    for i, (qh, kh) in enumerate(((0, 0), (1, 0), (1, 1))):
        dist = (qh - kh) * P + s - t
        for w, d in PATTERNS:
            mult[:, i * P:(i + 1) * P] += (dist >= 0) & (dist <= w) & (dist % d == 0)
    mask = np.where(mult > 0, np.float32(0), np.float32(NEG))
    rows = [*range(PAST - P, PAST), *range(512, PAST - P, 4), *range(0, 512, 16), PAST]
    smult = np.zeros(len(rows), np.float32)
    for w, d in PATTERNS:
        smult += np.array([PAST - r <= w and (PAST - r) % d == 0 for r in rows], np.float32)
    return [ident, ones, cum.astype(np.float32), level, mult, mask, np.tile(smult, (P, 1))]


def kernel(**inputs):
    import numpy as _np
    import concourse.bacc as _bacc
    from concourse import mybir as _mybir
    from concourse.bass_utils import run_bass_kernel_spmd as _run

    nc = _bacc.Bacc("TRN2", target_bir_lowering=False, num_devices=1)
    arrays, args = {}, []
    given = [(name, _np.ascontiguousarray(inputs[name])) for name in _INS]
    given += [(f"const_{i}", a) for i, a in enumerate(shape_constants())]
    for name, a in given:
        arrays[f"in_{name}_dram"] = a
        args.append(nc.dram_tensor(f"in_{name}_dram", a.shape, _mybir.dt.from_np(a.dtype), kind="ExternalInput").ap())
    for i, shape in enumerate(_OUTS):
        args.append(nc.dram_tensor(f"out_{i}_dram", shape, F32, kind="ExternalOutput").ap())
    layer_step(nc, *args)
    r = _run(nc, [arrays], core_ids=[0])
    return tuple(r.results[0][f"out_{i}_dram"] for i in range(len(_OUTS)))
```
